# Optimizing a Trainium2 kernel written in Bass

```python
import math
import jax, jax.numpy as jnp
from jax import lax
import numpy as np
import jax
import jax.numpy as jnp

D_MODEL = 1024
BATCH = 1
SEQ = 512
DEPTH = 1

N_META = 16
D_MIX = 2 * D_MODEL
D_SSD = D_MIX // 2
SSD_HEAD_DIM = 64
SSD_HEADS = D_SSD // SSD_HEAD_DIM
SSD_GROUPS = 2
SSD_HEADS_PER_GROUP = SSD_HEADS // SSD_GROUPS
SSD_STATE = 128
SSD_CONV = 4
SSD_CHUNK = 256
D_XBC = D_SSD + 2 * SSD_GROUPS * SSD_STATE
D_S5 = D_MIX - D_SSD
S5_GROUP_WIDTH = 16
S5_GROUPS = D_S5 // S5_GROUP_WIDTH
S5_STATE = 64
D_FF = 4 * D_MODEL
D_IN_PROJ = D_SSD + D_XBC + SSD_HEADS + D_S5
NORM_EPS = 1e-5
DT_MIN = 0.001
DT_MAX = 0.1


def _rmsnorm(x, g):
    xf = x.astype(jnp.float32)
    y = xf * lax.rsqrt(jnp.mean(xf * xf, axis=-1, keepdims=True) + NORM_EPS)
    return (y * g.astype(jnp.float32)).astype(x.dtype)

def _causal_depthwise_conv(x, w, b):
    k, c = w.shape
    y = lax.conv_general_dilated(x, w[:, None, :].astype(x.dtype), window_strides=(1,), padding=[(k - 1, 0)], dimension_numbers=('NWC', 'WIO', 'NWC'), feature_group_count=c)
    return y + b.astype(x.dtype)

def _ssd_mixer(xbc, dt_raw, z, dt_bias, a_log, d_skip, g_norm):
    bsz, length, _ = xbc.shape
    f32 = jnp.float32
    xbc = xbc.astype(f32)
    x_in = xbc[..., :D_SSD]
    b_in = xbc[..., D_SSD:D_SSD + SSD_GROUPS * SSD_STATE]
    c_in = xbc[..., D_SSD + SSD_GROUPS * SSD_STATE:]
    dt = jax.nn.softplus(dt_raw.astype(f32) + dt_bias.astype(f32))
    front = SSD_CHUNK - N_META
    n_real_chunks = -(-(length - N_META) // SSD_CHUNK)
    total = SSD_CHUNK * (1 + n_real_chunks)
    back = total - front - length
    pad = lambda t: jnp.pad(t, ((0, 0), (front, back), (0, 0)))
    n_chunks = total // SSD_CHUNK
    shp = (bsz, n_chunks, SSD_CHUNK, SSD_GROUPS)
    xc = pad(x_in).reshape(shp + (SSD_HEADS_PER_GROUP, SSD_HEAD_DIM))
    bc = pad(b_in).reshape(shp + (SSD_STATE,))
    cc = pad(c_in).reshape(shp + (SSD_STATE,))
    dtc = pad(dt).reshape(shp + (SSD_HEADS_PER_GROUP,))
    a = -jnp.exp(a_log.astype(f32)).reshape(SSD_GROUPS, SSD_HEADS_PER_GROUP)
    a_cs = jnp.cumsum(dtc * a, axis=2)
    xdt = xc * dtc[..., None]
    causal = jnp.tril(jnp.ones((SSD_CHUNK, SSD_CHUNK), dtype=bool))[:, :, None, None]
    seg = a_cs[:, :, :, None] - a_cs[:, :, None, :]
    decay = jnp.exp(jnp.where(causal, seg, -jnp.inf))
    cb = jnp.einsum('bclgn,bcsgn->bclsg', cc, bc)
    y_diag = jnp.einsum('bclsg,bclsgr,bcsgrp->bclgrp', cb, decay, xdt)
    decay_to_end = jnp.exp(a_cs[:, :, -1:] - a_cs)
    chunk_states = jnp.einsum('bclgn,bclgr,bclgrp->bcgrpn', bc, decay_to_end, xdt)
    chunk_decay = jnp.exp(a_cs[:, :, -1])

    def step(state, inp):
        dec, st = inp
        return state * dec[..., None, None] + st, state

    init = jnp.zeros((bsz, SSD_GROUPS, SSD_HEADS_PER_GROUP, SSD_HEAD_DIM, SSD_STATE), f32)
    _, prev = lax.scan(step, init, (jnp.moveaxis(chunk_decay, 1, 0), jnp.moveaxis(chunk_states, 1, 0)))
    prev = jnp.moveaxis(prev, 0, 1)
    y_off = jnp.einsum('bclgn,bcgrpn,bclgr->bclgrp', cc, prev, jnp.exp(a_cs))
    d = d_skip.astype(f32).reshape(SSD_GROUPS, SSD_HEADS_PER_GROUP, 1)
    y = (y_diag + y_off + xc * d).reshape(bsz, total, D_SSD)[:, front:front + length]
    y = y * jax.nn.silu(z.astype(f32))
    return _rmsnorm(y, g_norm)

def _s5_mixer(u, lam_re, lam_im, log_step, b_re, b_im, c_re, c_im, d_skip, w_glu, b_glu, g_norm):
    bsz, length, _ = u.shape
    f32 = jnp.float32
    u = u.astype(f32).reshape(bsz, length, S5_GROUPS, S5_GROUP_WIDTH)
    lr = lam_re.astype(f32)
    li = lam_im.astype(f32)
    step = jnp.exp(log_step.astype(f32))[:, None]
    mag = jnp.exp(lr * step)
    ab_re = mag * jnp.cos(li * step)
    ab_im = mag * jnp.sin(li * step)
    den = lr * lr + li * li
    coef_re = ((ab_re - 1.0) * lr + ab_im * li) / den
    coef_im = (ab_im * lr - (ab_re - 1.0) * li) / den
    br = b_re.astype(f32)
    bi = b_im.astype(f32)
    bb_re = coef_re[..., None] * br - coef_im[..., None] * bi
    bb_im = coef_re[..., None] * bi + coef_im[..., None] * br
    bu_re = jnp.einsum('blgh,gph->blgp', u, bb_re)
    bu_im = jnp.einsum('blgh,gph->blgp', u, bb_im)
    a_re = jnp.broadcast_to(ab_re, (1, length) + ab_re.shape)
    a_im = jnp.broadcast_to(ab_im, (1, length) + ab_im.shape)

    def combine(e_i, e_j):
        ar_i, ai_i, br_i, bi_i = e_i
        ar_j, ai_j, br_j, bi_j = e_j
        return (ar_j * ar_i - ai_j * ai_i,
                ar_j * ai_i + ai_j * ar_i,
                ar_j * br_i - ai_j * bi_i + br_j,
                ar_j * bi_i + ai_j * br_i + bi_j)

    _, _, s_re, s_im = lax.associative_scan(combine, (a_re, a_im, bu_re, bu_im), axis=1)
    y = (jnp.einsum('blgp,ghp->blgh', s_re, c_re.astype(f32))
         - jnp.einsum('blgp,ghp->blgh', s_im, c_im.astype(f32))
         + u * d_skip.astype(f32))
    y = jax.nn.gelu(y.reshape(bsz, length, D_S5), approximate=False)
    v = y @ w_glu.astype(f32) + b_glu.astype(f32)
    y = v[..., :D_S5] * jax.nn.sigmoid(v[..., D_S5:])
    return _rmsnorm(y, g_norm)

def first_inputs(seed: int = 0) -> dict:
    key = jax.random.key(seed)
    ks = jax.random.split(key, 32)
    f32 = jnp.float32
    nrm = lambda k, s, sc: jax.random.normal(k, s, f32) * sc
    gain = lambda k, s: 1.0 + 0.01 * jax.random.normal(k, s, f32)
    dt = jnp.exp(jax.random.uniform(ks[6], (DEPTH, SSD_HEADS), f32) * (math.log(DT_MAX) - math.log(DT_MIN)) + math.log(DT_MIN))
    dt = jnp.maximum(dt, 1e-4)
    dt_bias = dt + jnp.log(-jnp.expm1(-dt))
    n_idx = jnp.arange(S5_STATE, dtype=f32)
    return {
        'x': nrm(ks[0], (BATCH, SEQ, D_MODEL), 1.0),
        'meta_tokens': nrm(ks[1], (N_META, D_MODEL), 1.0),
        'g_mix': gain(ks[2], (DEPTH, D_MODEL)),
        'w_in': nrm(ks[3], (DEPTH, D_MODEL, D_IN_PROJ), D_MODEL ** -0.5),
        'conv_w': nrm(ks[4], (DEPTH, SSD_CONV, D_XBC), SSD_CONV ** -0.5),
        'conv_b': nrm(ks[5], (DEPTH, D_XBC), 0.01),
        'dt_bias': dt_bias,
        'a_log': jnp.log(jax.random.uniform(ks[7], (DEPTH, SSD_HEADS), f32, 1.0, 16.0)),
        'd_ssd': gain(ks[8], (DEPTH, SSD_HEADS)),
        'g_ssd': gain(ks[9], (DEPTH, D_SSD)),
        'lam_re': -0.5 + nrm(ks[10], (DEPTH, S5_GROUPS, S5_STATE), 0.01),
        'lam_im': math.pi * n_idx + nrm(ks[11], (DEPTH, S5_GROUPS, S5_STATE), 0.01),
        'log_step': jax.random.uniform(ks[12], (DEPTH, S5_GROUPS), f32, math.log(DT_MIN), math.log(DT_MAX)),
        'b_re': nrm(ks[13], (DEPTH, S5_GROUPS, S5_STATE, S5_GROUP_WIDTH), (2 * S5_GROUP_WIDTH) ** -0.5),
        'b_im': nrm(ks[14], (DEPTH, S5_GROUPS, S5_STATE, S5_GROUP_WIDTH), (2 * S5_GROUP_WIDTH) ** -0.5),
        'c_re': nrm(ks[15], (DEPTH, S5_GROUPS, S5_GROUP_WIDTH, S5_STATE), S5_STATE ** -0.5),
        'c_im': nrm(ks[16], (DEPTH, S5_GROUPS, S5_GROUP_WIDTH, S5_STATE), S5_STATE ** -0.5),
        'd_s5': nrm(ks[17], (DEPTH, S5_GROUPS, S5_GROUP_WIDTH), 1.0),
        'w_glu': nrm(ks[18], (DEPTH, D_S5, 2 * D_S5), D_S5 ** -0.5),
        'b_glu': nrm(ks[19], (DEPTH, 2 * D_S5), 0.01),
        'g_s5': gain(ks[20], (DEPTH, D_S5)),
        'w_out': nrm(ks[21], (DEPTH, D_MIX, D_MODEL), D_MIX ** -0.5),
        'g_mlp': gain(ks[22], (DEPTH, D_MODEL)),
        'w_up': nrm(ks[23], (DEPTH, D_MODEL, D_FF), D_MODEL ** -0.5),
        'w_down': nrm(ks[24], (DEPTH, D_FF, D_MODEL), D_FF ** -0.5),
        'g_final': gain(ks[25], (D_MODEL,)),
    }

def first_block(x, meta_tokens, g_mix, w_in, conv_w, conv_b, dt_bias, a_log, d_ssd, g_ssd, lam_re, lam_im, log_step, b_re, b_im, c_re, c_im, d_s5, w_glu, b_glu, g_s5, w_out, g_mlp, w_up, w_down, g_final):
    bsz = x.shape[0]
    meta = jnp.broadcast_to(meta_tokens.astype(x.dtype)[None], (bsz, N_META, D_MODEL))
    h = jnp.concatenate([meta, x], axis=1)
    o_xbc = D_SSD
    o_dt = D_SSD + D_XBC
    o_u = o_dt + SSD_HEADS
    for layer in range(DEPTH):
        n = _rmsnorm(h, g_mix[layer])
        proj = n @ w_in[layer]
        z = proj[..., :o_xbc]
        xbc = jax.nn.silu(_causal_depthwise_conv(proj[..., o_xbc:o_dt], conv_w[layer], conv_b[layer]))
        dt_raw = proj[..., o_dt:o_u]
        u = proj[..., o_u:]
        y_ssd = _ssd_mixer(xbc, dt_raw, z, dt_bias[layer], a_log[layer], d_ssd[layer], g_ssd[layer])
        y_s5 = _s5_mixer(u, lam_re[layer], lam_im[layer], log_step[layer], b_re[layer], b_im[layer], c_re[layer], c_im[layer], d_s5[layer], w_glu[layer], b_glu[layer], g_s5[layer])
        mix = jnp.concatenate([y_ssd.astype(h.dtype), y_s5.astype(h.dtype)], axis=-1)
        h = h + mix @ w_out[layer]
        m = _rmsnorm(h, g_mlp[layer]) @ w_up[layer]
        h = h + jnp.square(jax.nn.relu(m)) @ w_down[layer]
    return _rmsnorm(h, g_final)[:, N_META:].astype(x.dtype)


_first_inputs = first_inputs


def first_inputs(seed=0):
    import zlib

    import numpy as np

    out = dict(_first_inputs(seed))
    spreads = {}
    factors = {}
    for name, (base, spread) in spreads.items():
        noise = np.random.default_rng([zlib.crc32(name.encode()), seed]).standard_normal(out[name].shape)
        drawn = base * np.exp(spread * noise) if base else spread * noise
        out[name] = __import__('jax').numpy.asarray(drawn.astype(out[name].dtype))
    for name, factor in factors.items():
        out[name] = (out[name] * factor).astype(out[name].dtype)
    return out


_narrow_inputs = first_inputs


def first_inputs(seed=0):
    out = dict(_narrow_inputs(seed))
    wider = {'g_mix': 6.23,
     'conv_b': 8.06,
     'd_ssd': 12.0,
     'g_ssd': 11.97,
     'lam_re': 12.0,
     'b_glu': 7.48,
     'g_s5': 12.0,
     'g_mlp': 8.42,
     'g_final': 6.32}
    for name, times in wider.items():
        mean = out[name].mean()
        out[name] = (mean + times * (out[name] - mean)).astype(out[name].dtype)
    return out


DEPTH_2 = 2

CTX_LEN = 256
GRID_W = 64
CONV_DIM = 512
CONV_K = 31
NA_HEADS = 8
HEAD_DIM = 64
NA_DIM = NA_HEADS * HEAD_DIM
NA_KH_MAX = 8
NA_KW = 16
ROPE_THETA = 10000.0
FFN_DIM = 2816
FFN_CONV_K = 3
N_BRANCH = 2
EPS = 1e-6
GLU_END = 2 * CONV_DIM
QKV_END = GLU_END + 3 * NA_DIM
IN_DIM = QKV_END + N_BRANCH * D_MODEL


def rmsnorm(x, g):
    xf = x.astype(jnp.float32)
    y = xf * lax.rsqrt(jnp.mean(xf * xf, axis=-1, keepdims=True) + EPS)
    return (y * g.astype(jnp.float32)).astype(x.dtype)

def layernorm(x, g, b):
    xf = x.astype(jnp.float32)
    mu = jnp.mean(xf, axis=-1, keepdims=True)
    var = jnp.mean(jnp.square(xf - mu), axis=-1, keepdims=True)
    y = (xf - mu) * lax.rsqrt(var + EPS)
    return (y * g.astype(jnp.float32) + b.astype(jnp.float32)).astype(x.dtype)

def modulate(h, shift, scale):
    return h * (1 + scale) + shift

def dwconv1d(x, w, b):
    k, ch = w.shape
    y = lax.conv_general_dilated(
        x, w.astype(x.dtype)[:, None, :], window_strides=(1,),
        padding=[(k // 2, k // 2)],
        dimension_numbers=("NWC", "WIO", "NWC"),
        feature_group_count=ch)
    return y + b

def split_heads(t):
    b, l, _ = t.shape
    return t.reshape(b, l, NA_HEADS, HEAD_DIM).transpose(0, 2, 1, 3)

def merge_heads(t):
    b, h, l, d = t.shape
    return t.transpose(0, 2, 1, 3).reshape(b, l, h * d)

def rope_2d(x, pos_row, pos_col):
    half = HEAD_DIM // 2
    inv_freq = ROPE_THETA ** (-jnp.arange(0, half, 2, dtype=jnp.float32) / half)

    def rot(xa, pos):
        ang = pos[:, None] * inv_freq[None, :]
        cos, sin = jnp.cos(ang), jnp.sin(ang)
        x1, x2 = jnp.split(xa.astype(jnp.float32), 2, axis=-1)
        return jnp.concatenate([x1 * cos - x2 * sin, x1 * sin + x2 * cos], axis=-1)

    out = jnp.concatenate([rot(x[..., :half], pos_row), rot(x[..., half:], pos_col)], axis=-1)
    return out.astype(x.dtype)

def conv_branch(p_glu, dw, dw_b, ln_g, ln_b, w_o):
    a, g = jnp.split(p_glu, 2, axis=-1)
    u = a * jax.nn.sigmoid(g)
    u = dwconv1d(u, dw, dw_b)
    u = jax.nn.silu(layernorm(u, ln_g, ln_b))
    return u @ w_o

def neighbourhood_attention(q, k, v, k_ctx, v_ctx, rpb):
    b, h, l, dh = q.shape
    rows = l // GRID_W
    kh = min(NA_KH_MAX, rows)
    n_win = kh * NA_KW
    qg = q.reshape(b, h, rows, GRID_W, dh)
    kg = k.reshape(b, h, rows, GRID_W, dh)
    vg = v.reshape(b, h, rows, GRID_W, dh)
    cols = jnp.arange(GRID_W)
    col_start = jnp.clip(cols - NA_KW // 2, 0, GRID_W - NA_KW)
    col_idx = col_start[:, None] + jnp.arange(NA_KW)[None, :]
    dc_idx = col_idx - cols[:, None] + (NA_KW - 1)
    scale = HEAD_DIM ** -0.5

    def row_block(r):
        row_start = jnp.clip(r - kh // 2, 0, rows - kh)
        q_r = lax.dynamic_index_in_dim(qg, r, axis=2, keepdims=False)
        k_band = lax.dynamic_slice_in_dim(kg, row_start, kh, axis=2)
        v_band = lax.dynamic_slice_in_dim(vg, row_start, kh, axis=2)
        k_win = k_band[:, :, :, col_idx]
        v_win = v_band[:, :, :, col_idx]
        s_win = jnp.einsum("bhqd,bhiqjd->bhqij", q_r, k_win,
                           preferred_element_type=jnp.float32) * scale
        dr_idx = row_start + jnp.arange(kh) - r + (NA_KH_MAX - 1)
        bias = rpb[:, dr_idx[None, :, None], dc_idx[:, None, :]]
        s_win = s_win + bias[None].astype(jnp.float32)
        s_ctx = jnp.einsum("bhqd,bhcd->bhqc", q_r, k_ctx,
                           preferred_element_type=jnp.float32) * scale
        s = jnp.concatenate([s_win.reshape(b, h, GRID_W, n_win), s_ctx], axis=-1)
        p = jax.nn.softmax(s, axis=-1).astype(v.dtype)
        p_win = p[..., :n_win].reshape(b, h, GRID_W, kh, NA_KW)
        p_ctx = p[..., n_win:]
        return (jnp.einsum("bhqij,bhiqjd->bhqd", p_win, v_win)
                + jnp.einsum("bhqc,bhcd->bhqd", p_ctx, v_ctx))

    out = lax.map(row_block, jnp.arange(rows))
    return out.transpose(1, 2, 0, 3, 4).reshape(b, h, l, dh)

def context_attention(q, k, v):
    s = jnp.einsum("bhqd,bhkd->bhqk", q, k, preferred_element_type=jnp.float32) * (HEAD_DIM ** -0.5)
    p = jax.nn.softmax(s, axis=-1).astype(v.dtype)
    return jnp.einsum("bhqk,bhkd->bhqd", p, v)

def gated_merge(p_gate, y_conv, y_attn, w_o):
    g_conv, g_attn = jnp.split(jax.nn.sigmoid(p_gate), 2, axis=-1)
    return (g_conv * y_conv + g_attn * y_attn) @ w_o

def conv_ffn(h, w_up, dw, dw_b, w_down):
    u = dwconv1d(h @ w_up, dw, dw_b)
    a, g = jnp.split(u, 2, axis=-1)
    return (jax.nn.silu(g) * a) @ w_down

def second_inputs(seed: int = 0) -> dict:
    key = jax.random.key(seed)
    ks = jax.random.split(key, 24)
    n = jax.random.normal
    f32 = jnp.float32
    D = D_MODEL
    return {
        "x": n(ks[0], (BATCH, SEQ, D), f32),
        "c": n(ks[1], (BATCH, D), f32),
        "ctx": n(ks[2], (BATCH, CTX_LEN, D), f32),
        "c_ctx": n(ks[3], (D,), f32),
        "w_ada": n(ks[4], (DEPTH_2, D, 6 * D), f32) * (0.5 * D ** -0.5),
        "b_ada": n(ks[5], (DEPTH_2, 6 * D), f32) * 0.02,
        "norm1_g": 1.0 + 0.02 * n(ks[6], (DEPTH_2, D), f32),
        "w_in": n(ks[7], (DEPTH_2, D, IN_DIM), f32) * D ** -0.5,
        "conv_dw": n(ks[8], (DEPTH_2, CONV_K, CONV_DIM), f32) * CONV_K ** -0.5,
        "conv_dw_b": n(ks[9], (DEPTH_2, CONV_DIM), f32) * 0.02,
        "conv_ln_g": 1.0 + 0.02 * n(ks[10], (DEPTH_2, CONV_DIM), f32),
        "conv_ln_b": n(ks[11], (DEPTH_2, CONV_DIM), f32) * 0.02,
        "w_conv_out": n(ks[12], (DEPTH_2, CONV_DIM, D), f32) * CONV_DIM ** -0.5,
        "na_rpb": n(ks[13], (DEPTH_2, NA_HEADS, 2 * NA_KH_MAX - 1, 2 * NA_KW - 1), f32) * 0.1,
        "w_na_out": n(ks[14], (DEPTH_2, NA_DIM, D), f32) * NA_DIM ** -0.5,
        "w_out": n(ks[15], (DEPTH_2, D, D), f32) * D ** -0.5,
        "norm2_g": 1.0 + 0.02 * n(ks[16], (DEPTH_2, D), f32),
        "w_up": n(ks[17], (DEPTH_2, D, 2 * FFN_DIM), f32) * D ** -0.5,
        "ffn_dw": n(ks[18], (DEPTH_2, FFN_CONV_K, 2 * FFN_DIM), f32) * FFN_CONV_K ** -0.5,
        "ffn_dw_b": n(ks[19], (DEPTH_2, 2 * FFN_DIM), f32) * 0.02,
        "w_down": n(ks[20], (DEPTH_2, FFN_DIM, D), f32) * FFN_DIM ** -0.5,
        "final_norm_g": 1.0 + 0.02 * n(ks[21], (D,), f32),
    }

def second_block(x, c, ctx, c_ctx, w_ada, b_ada, norm1_g, w_in, conv_dw, conv_dw_b, conv_ln_g,
              conv_ln_b, w_conv_out, na_rpb, w_na_out, w_out, norm2_g, w_up, ffn_dw, ffn_dw_b,
              w_down, final_norm_g):
    L = x.shape[1]
    t = jnp.arange(L)
    pos_row = (t // GRID_W).astype(jnp.float32)
    pos_col = (t % GRID_W).astype(jnp.float32)
    xc = ctx
    s_lat = jax.nn.silu(c)
    s_ctx = jax.nn.silu(c_ctx)
    for l in range(DEPTH_2):
        last = l == DEPTH_2 - 1
        mod = (s_lat @ w_ada[l] + b_ada[l])[:, None, :]
        sh1, sc1, g1, sh2, sc2, g2 = jnp.split(mod, 6, axis=-1)
        mod_c = s_ctx @ w_ada[l] + b_ada[l]
        csh1, csc1, cg1, csh2, csc2, cg2 = jnp.split(mod_c, 6, axis=-1)

        h = modulate(rmsnorm(x, norm1_g[l]), sh1, sc1)
        hc = modulate(rmsnorm(xc, norm1_g[l]), csh1, csc1)
        p = h @ w_in[l]
        if last:
            kv_c = hc @ w_in[l][:, GLU_END + NA_DIM:QKV_END]
            k_c, v_c = (split_heads(u) for u in jnp.split(kv_c, 2, axis=-1))
        else:
            pc = hc @ w_in[l]
            q_c, k_c, v_c = (split_heads(u) for u in jnp.split(pc[..., GLU_END:QKV_END], 3, axis=-1))

        q, k, v = (split_heads(u) for u in jnp.split(p[..., GLU_END:QKV_END], 3, axis=-1))
        q = rope_2d(q, pos_row, pos_col)
        k = rope_2d(k, pos_row, pos_col)
        y_conv = conv_branch(p[..., :GLU_END], conv_dw[l], conv_dw_b[l], conv_ln_g[l],
                             conv_ln_b[l], w_conv_out[l])
        y_attn = merge_heads(neighbourhood_attention(q, k, v, k_c, v_c, na_rpb[l])) @ w_na_out[l]
        x = x + g1 * gated_merge(p[..., QKV_END:], y_conv, y_attn, w_out[l])

        h2 = modulate(rmsnorm(x, norm2_g[l]), sh2, sc2)
        x = x + g2 * conv_ffn(h2, w_up[l], ffn_dw[l], ffn_dw_b[l], w_down[l])

        if not last:
            yc_conv = conv_branch(pc[..., :GLU_END], conv_dw[l], conv_dw_b[l], conv_ln_g[l],
                                  conv_ln_b[l], w_conv_out[l])
            yc_attn = merge_heads(context_attention(q_c, k_c, v_c)) @ w_na_out[l]
            xc = xc + cg1 * gated_merge(pc[..., QKV_END:], yc_conv, yc_attn, w_out[l])
            hc2 = modulate(rmsnorm(xc, norm2_g[l]), csh2, csc2)
            xc = xc + cg2 * conv_ffn(hc2, w_up[l], ffn_dw[l], ffn_dw_b[l], w_down[l])
    return rmsnorm(x, final_norm_g)


def setup_inputs(seed=0):
    out = dict(first_inputs(seed))
    for name, value in second_inputs(seed + 1).items():
        if name != "x":
            out[name + "_2"] = value
    return out


def reference(
    x, meta_tokens, g_mix, w_in, conv_w, conv_b, dt_bias, a_log, d_ssd, g_ssd, lam_re, lam_im,
    log_step, b_re, b_im, c_re, c_im, d_s5, w_glu, b_glu, g_s5, w_out, g_mlp, w_up, w_down,
    g_final, c_2, ctx_2, c_ctx_2, w_ada_2, b_ada_2, norm1_g_2, w_in_2, conv_dw_2, conv_dw_b_2,
    conv_ln_g_2, conv_ln_b_2, w_conv_out_2, na_rpb_2, w_na_out_2, w_out_2, norm2_g_2, w_up_2,
    ffn_dw_2, ffn_dw_b_2, w_down_2, final_norm_g_2,
):
    x = first_block(
        x, meta_tokens, g_mix, w_in, conv_w, conv_b, dt_bias, a_log, d_ssd, g_ssd, lam_re,
        lam_im, log_step, b_re, b_im, c_re, c_im, d_s5, w_glu, b_glu, g_s5, w_out, g_mlp, w_up,
        w_down, g_final,
    )
    return second_block(
        x, c_2, ctx_2, c_ctx_2, w_ada_2, b_ada_2, norm1_g_2, w_in_2, conv_dw_2, conv_dw_b_2,
        conv_ln_g_2, conv_ln_b_2, w_conv_out_2, na_rpb_2, w_na_out_2, w_out_2, norm2_g_2,
        w_up_2, ffn_dw_2, ffn_dw_b_2, w_down_2, final_norm_g_2,
    )


_drawn_inputs = setup_inputs


def setup_inputs(seed=0):
    import zlib

    import numpy as np

    out = dict(_drawn_inputs(seed))
    spreads = {}
    factors = {'lam_re': 6.675,
     'ctx_2': 2.748,
     'norm1_g_2': 8.0,
     'conv_dw_b_2': 8.0,
     'conv_ln_g_2': 8.0,
     'conv_ln_b_2': 8.0,
     'na_rpb_2': 8.0,
     'norm2_g_2': 6.392,
     'ffn_dw_b_2': 6.896,
     'final_norm_g_2': 2.837}
    for name, (base, spread) in spreads.items():
        noise = np.random.default_rng([zlib.crc32(name.encode()), seed]).standard_normal(out[name].shape)
        drawn = base * np.exp(spread * noise) if base else spread * noise
        out[name] = jnp.asarray(drawn.astype(out[name].dtype))
    for name, factor in factors.items():
        out[name] = (out[name] * factor).astype(out[name].dtype)
    return out
```

```python
import math

import numpy as np

import concourse.bass as bass
import concourse.mybir as mybir
from concourse.alu_op_type import AluOpType as ALU

F32 = mybir.dt.float32
F32R = mybir.dt.float32r
ACT = mybir.ActivationFunctionType
AX = mybir.AxisListType

P = 128
DM = 1024
NT = DM // P
SEQ, N_META = 512, 16
TM = SEQ + N_META
HALF = TM // 2
SSD_HEADS, HEAD, STATE = 16, 64, 128
XBC_TILES = (DM + 4 * STATE) // P
CHUNK = 128
NCH = 5
FRONT = NCH * CHUNK - TM
S5_G, S5_H, S5_P = 64, 16, 64
LB = 8
NB = TM // LB
NB0 = N_META // LB
NPAIR = S5_G // 2
FF1 = 4 * DM
CTX = 256
CONV, KTAP = 512, 31
PADT = KTAP // 2
POOL_TAPS = 22
NH, DH = 8, 64
FF2_TILES = 22
CHUNKS2 = [(0, 8), (8, 8), (16, 6)]
GW, GH = 64, 8
NEG = -1e30
ROUND = 12582912.0
TWO_PI_HI, TWO_PI_LO = 6.28125, 2 * math.pi - 6.28125
R = 4
CREDIT = 4

U_U, U_DT, U_XBC, U_Z = 0, 8, 9, 21
U_OUT1, U_GLU, U_OUT2, U_FF = 29, 37, 53, 61
N_B1 = U_FF + 4 * 16
N_ADA = 2 * 48
U_ADA = U_GLU + R
N_LAYER = 20 + 24 + 8 + 16 + 8 + 16 + 8 + 12 + 8
N_UNITS = N_B1 + 3 * N_LAYER + 8

WIN_AT = [0, 1, 3, 4]
MIX = {2: (4, 0), 3: (5, 1)}

VEC = {}


def vec_layout():
    at = 0
    for name, n in ([("g_mix", 8), ("cw0", 12), ("cw1", 12), ("cw2", 12), ("cw3", 12), ("cb", 12),
                     ("dtb", 1), ("alog", 1), ("dskip", 8), ("g_ssd", 8), ("b_glu", 16), ("g_s5", 8),
                     ("g_mlp", 8), ("g_final", 8), ("gf2", 8), ("c", 16), ("eps5", 1), ("eps6", 1), ("halfpi", 1), ("one", 1)]
                    + [(f"{n}{l}", k) for l in range(2) for n, k in
                       (("bada", 48), ("n1", 8), ("n2", 8), ("dw", 4 * KTAP), ("dwb", 4), ("lng", 4), ("lnb", 4),
                        ("fw0", 44), ("fw1", 44), ("fw2", 44), ("fb", 44))]):
        VEC[name] = (at, n)
        at += n
    return at


NVEC = vec_layout()
CONST = {"ident": 0, "ones": 128, "ones512": 256, "tri": 384, "rot": 512, "cos": 640, "sin": 1152, "keep": 1664}
NCONST = 1664 + NCH * CHUNK


class Steps:

    def __init__(self, sem, names, first=0):
        self.sem, self.names, self.n = sem, names, len(names)
        self.first, self.taken = first, 0

    def part(self, passes):
        s = Steps(self.sem, self.names, self.taken)
        self.taken += passes
        return s

    def credit(self, eng):
        eng.nop().then_inc(self.sem, CREDIT * self.n)

    def past(self, step, i=0, back=0):
        return (i + (self.first + CREDIT - back)) * self.n + self.names.index(step) + 1


def build(nc, A, out):
    base, K = 16640, 1024

    def at(name, shape, offset, dt=F32):
        assert base + offset + int(np.prod(shape[1:])) * 4 <= 229368, name
        return nc.alloc_sbuf_tensor_at(name, shape, dt, offset=base + offset, align_bytes=4)

    def sem(name):
        return nc.alloc_semaphore(name)

    def steps(name, *names):
        s = Steps(sem(name), names)
        every_steps.append(s)
        return s

    every_steps = []
    wraw = at("wraw", [P, R, 8, P], 0)
    whi = at("whi", [P, R, 8, P], 16 * K, F32R)
    wlo = at("wlo", [P, R, 8, P], 32 * K, F32R)
    O_H, O_HC, O_X = 48 * K, 64 * K, 72 * K
    res = at("res", [P, NT, SEQ], O_H)
    resc = at("resc", [P, NT, CTX], O_HC)
    XB = NT * TM * 4
    xhi = at("xhi", [P, NT, TM], O_X, F32R)
    xlo = at("xlo", [P, NT, TM], O_X + XB, F32R)
    O_HH = O_X + 2 * XB
    O_HL = O_HH + 16 * K
    hhi = at("hhi", [P, NT, SEQ], O_HH, F32R)
    hlo = at("hlo", [P, NT, SEQ], O_HL, F32R)
    O_C = O_HL + 16 * K
    cst = at("cst", [P, NCONST], O_C)
    O_V = O_C + NCONST * 4
    vec = at("vec", [P, NVEC], O_V)
    O_M = O_V + NVEC * 4
    mod = at("mod", [P, 2, 48, 2], O_M)
    cs = at("cs", [P, 8, 2], O_M + 768)
    gm = at("gm", [P, 2, 2, 8, 2], O_M + 832)
    O_KC = O_M + 832 + 256
    kctx = at("kctx", [P, 4, CTX], O_KC)
    vctx = at("vctx", [P, 2, CONV], O_KC + 4 * K)
    SC = O_KC + 8 * K
    ps = nc.alloc_psum_tensor("ps", [P, 8, 512], F32)

    ident = cst[:, CONST["ident"]:CONST["ident"] + P]
    ones = cst[:, CONST["ones"]:CONST["ones"] + P]
    ones512 = cst[:, CONST["ones512"]:CONST["ones512"] + P]
    tri = cst[:, CONST["tri"]:CONST["tri"] + P]
    rot = cst[:, CONST["rot"]:CONST["rot"] + P]
    cosT = cst[:, CONST["cos"]:CONST["cos"] + SEQ]
    sinT = cst[:, CONST["sin"]:CONST["sin"] + SEQ]
    keep = cst[0:16, CONST["keep"]:CONST["keep"] + NCH * CHUNK]

    def col(name, k=0):
        return vec[:, bass.ds(VEC[name][0] + k, 1)]

    def colr(name, n, k=0):
        return vec[:, VEC[name][0] + k:VEC[name][0] + k + n]

    landed = [sem(f"w_landed{s}") for s in range(R)]
    hi_done = [sem(f"w_hi{s}") for s in range(R)]
    lo_done = [sem(f"w_lo{s}") for s in range(R)]
    unit_done = [sem(f"unit_done{s}") for s in range(R)]
    acc_free = [sem(f"acc_free{s}") for s in range(R)]
    s_in = sem("inputs_landed")
    s_cst = sem("const_landed")
    s_out = sem("out_landed")

    def slot(g, i=0, rb=0):
        return g % R, g // R + i * rb

    def raw_round(g, i=0, rb=0):
        return slot(g, i, rb)[1] + (N_ADA // R if g >= U_ADA else 0)

    def loop(eng, n, body):
        if n == 1:
            body(0)
        else:
            with eng.Fori(0, n) as i:
                body(i)

    def acc(s, T):
        return ps[:, 2 * s, 0:T] if T <= 512 else ps[:, 2 * s:2 * s + 2, 0:HALF]

    def flat(ap, T):
        return ap if T <= 512 else ap.rearrange("p (a b) -> p a b", a=2)

    def split_hi(act, g, i=0, rb=0):
        if g >= N_UNITS:
            return
        s, rnd = slot(g, i, rb)
        act.wait_ge(landed[s], (raw_round(g, i, rb) + 1) * 16)
        act.wait_ge(unit_done[s], rnd + 1)
        act.activation(whi[:, s], wraw[:, s], ACT.Copy).then_inc(hi_done[s], 1)

    def split_lo(pool, g, i=0, rb=0):
        if g >= N_UNITS:
            return
        s, rnd = slot(g, i, rb)
        pool.wait_ge(hi_done[s], rnd + 1)
        pool.tensor_tensor(wlo[:, s], wraw[:, s], whi[:, s].bitcast(F32), ALU.subtract).then_inc(lo_done[s], 1)

    def pool_units(pool, U, n, per=4):
        def body(i):
            for j in range(per):
                split_lo(pool, U + j + R, i, per // R)
        loop(pool, n, body)

    def act_units(act, U, n, per=4):
        def body(i):
            for j in range(per):
                split_hi(act, U + j + R, i, per // R)
        loop(act, min(n, (N_UNITS - R - U) // per), body)

    def pe_unit(pe, g, i, rb, xh, xl, T, nk=8, ready=None, dual=False, wide=False, c0=0):
        s, rnd = slot(g, i, rb)
        pe.wait_ge(lo_done[s], raw_round(g if g < U_GLU else g + R, i, rb) + (1 if g < U_GLU else 0))
        pe.wait_ge(acc_free[s], rnd + 1)
        parts = [(s, 0, T)] if not wide else [(2 * s, 0, T)] if T <= 512 else [(2 * s, 0, HALF), (2 * s + 1, HALF, TM)]
        last = None
        for kt in range(nk):
            if ready is not None:
                ready(kt)
            first, end = kt == 0, kt == nk - 1
            if dual:
                parts = [(s + R * (kt // 4), 0, T)]
                first, end = kt % 4 == 0, kt % 4 == 3
            for bank, a, b in parts:
                o = ps[:, bank, 0:b - a]
                pe.matmul(o, whi[:, s, kt], xh[:, kt, c0 + a:c0 + b], start=first, stop=False)
                pe.matmul(o, whi[:, s, kt], xl[:, kt, c0 + a:c0 + b], start=False, stop=False)
                last = pe.matmul(o, wlo[:, s, kt], xh[:, kt, c0 + a:c0 + b], start=False, stop=end)
        last.then_inc(unit_done[s], 1)

    def read_out(g, i=0, rb=0, back=0):
        return slot(g, i, rb)[1] + 2 - back

    def all_freed(eng, U):
        for s in range(R):
            eng.wait_ge(acc_free[s], (U - 1 - s) // R + 2 if U > s else 1)

    NS = SC + 32 * K
    nsq = at("nsq", [P, 2, TM], NS)
    nacc = at("nacc", [P, TM], NS + 8 * TM)
    nrs = at("nrs", [P, TM], NS + 12 * TM)
    ntt = at("ntt", [P, 2, TM], NS + 16 * TM)
    n_sq, n_acc, n_sum, n_root, n_t, n_hi, n_lo, n_fin = (
        steps("norm_square", "sq"), steps("norm_squares_added", "acc"), steps("norm_sum", "sum"),
        steps("norm_root", "root"), steps("norm_scaled", "t"), steps("norm_hi", "hi"),
        steps("norm_lo", "lo"), steps("norm_in_place", "fin"))

    def norm_act(act, n, src, T, eps, ready=None, split=True, shift=None, dst=None):
        for kt in range(NT):
            if ready is not None:
                ready(act, kt)
            if kt >= 2 or n:
                act.wait_ge(n_acc.sem, n_acc.past("acc", n * NT + kt - 2))
            act.activation(nsq[:, kt % 2, 0:T], src(kt), ACT.Square).then_inc(n_sq.sem, 1)
        act.wait_ge(n_sum.sem, n_sum.past("sum", n))
        o = nrs[:, 0:T]
        act.activation(flat(o, T), ps[:, 6:8, 0:HALF] if T > 512 else ps[:, 7, 0:T], ACT.Sqrt,
                                  bias=col(eps)).then_inc(n_root.sem, 1)
        if split:
            for kt in range(NT):
                act.wait_ge(n_t.sem, n_t.past("t", hi_before[n] + kt))
                b = shift(kt) if shift else 0.0
                act.activation((dst or (xhi, xlo))[0][:, kt, 0:T], ntt[:, kt % 2, 0:T], ACT.Identity, bias=b).then_inc(n_hi.sem, 1)

    def norm_pe(pe, n, T):
        pe.wait_ge(n_acc.sem, n_acc.past("acc", n * NT + NT - 1))
        if T > 512:
            pe.matmul(ps[:, 6, 0:HALF], ones, nacc[:, 0:HALF], start=True, stop=True)
            last = pe.matmul(ps[:, 7, 0:HALF], ones, nacc[:, HALF:TM], start=True, stop=True)
        else:
            last = pe.matmul(ps[:, 7, 0:T], ones, nacc[:, 0:T], start=True, stop=True)
        last.then_inc(n_sum.sem, 1)

    def norm_dve(dve, n, src, T, gain, split=True, shift=None, dst=None):
        a = nacc[:, 0:T]
        for kt in range(NT):
            dve.wait_ge(n_sq.sem, n_sq.past("sq", n * NT + kt))
            if kt == 0:
                dve.tensor_copy(a, nsq[:, 0, 0:T]).then_inc(n_acc.sem, 1)
            else:
                dve.drain()
                dve.tensor_tensor(a, a, nsq[:, kt % 2, 0:T], ALU.add).then_inc(n_acc.sem, 1)
        dve.wait_ge(n_root.sem, n_root.past("root", n))
        r = nrs[:, 0:T]
        dve.reciprocal(r, r)
        dve.drain()
        if not split:
            for kt in range(NT):
                dve.scalar_tensor_tensor(src(kt), src(kt), gain(kt), r, ALU.mult, ALU.mult).then_inc(n_fin.sem, 1)
            dve.drain()
            return
        yhi, ylo = dst or (xhi, xlo)
        h0 = hi_before[n]
        t = lambda kt: ntt[:, kt % 2, 0:T]

        def scaled(kt):
            dve.scalar_tensor_tensor(t(kt), src(kt), gain(kt), r, ALU.mult, ALU.mult).then_inc(n_t.sem, 1)

        scaled(0)
        for kt in range(NT):
            if kt + 1 < NT:
                dve.drain()
                scaled(kt + 1)
            dve.wait_ge(n_hi.sem, n_hi.past("hi", h0 + kt))
            b = shift(kt) if shift else 0.0
            dve.scalar_tensor_tensor(ylo[:, kt, 0:T], t(kt), b, yhi[:, kt, 0:T].bitcast(F32),
                                              ALU.add, ALU.subtract).then_inc(n_lo.sem, 1)
        dve.drain()

    NORM = {"mix": 0, "ssd": 1, "s5": 2, "mlp": 3, "final1": 4, "c0a": 5, "c0b": 6, "l0a": 7, "l0b": 8,
            "c1a": 9, "l1a": 10, "l1b": 11, "final2": 12}
    hi_before, done = [], 0
    for name in NORM:
        hi_before.append(done)
        done += 0 if "final" in name else NT

    def normed(name):
        return lambda pe: (lambda kt: pe.wait_ge(n_lo.sem, n_lo.past("lo", hi_before[NORM[name]] + kt)))

    TB = O_KC
    xin = at("xin", [P, NT, TM], O_HH)
    cin = at("cin", [P, 2, 3 + TM + 1], O_HH)
    cac = at("cac", [P, 2, TM], O_HH + 8 * (TM + 4))
    zs = at("zs", [P, NT, SEQ], O_HL)
    uT = at("uT", [P, NT, TM], SC)
    xbc = at("xbc", [P, XBC_TILES, NCH * CHUNK], SC + 4 * NT * TM)
    ad = at("ad", [16, 2, NCH * CHUNK], TB)
    ads = at("ads", [16, 2, CHUNK], TB + 5120)
    sp1 = at("sp1", [16, 2], TB + 6144)
    adt = at("adt", [P, 2, 16], TB + 6208)
    dte = at("dte", [P, 16], TB + 6400)
    dtx = at("dtx", [16, TM], O_H)
    dty = at("dty", [16, TM], O_H + 4096)

    s_conv = steps("conv", "conv")
    s_cz = sem("conv_pads_zero")
    s_dta, s_dtd = steps("dt_scalar", "exp", "ln"), steps("dt_vector", "absneg", "dt")
    
    s_xbc = steps("xbc_ready", "x")

    def proj_pe(pe):
        ready = normed("mix")(pe)
        loop_u = lambda base, n, T, c0=0: loop(pe, n, lambda i: [
            pe_unit(pe, base + j, i, 1, xhi, xlo, T, wide=True, c0=c0) for j in range(4)])
        for kt in range(NT):
            ready(kt)
        loop_u(U_U, 2, TM)
        pe_unit(pe, U_DT, 0, 0, xhi, xlo, TM, wide=True)
        loop_u(U_XBC, 3, TM)
        loop_u(U_Z, 2, SEQ, N_META)

    def proj_act(act):
        def u_body(i):
            for j in range(4):
                s, rnd = slot(U_U + j, i, 1)
                act.wait_ge(unit_done[s], rnd + 2)
                act.activation(flat(uT[:, i * 4 + j], TM), acc(s, TM), ACT.Copy).then_inc(acc_free[s], 1)
                split_hi(act, U_U + j + R, i, 1)
        loop(act, 2, u_body)
        s, rnd = slot(U_DT)
        act.wait_ge(unit_done[s], rnd + 2)
        act.activation(flat(dtx[:, :], TM), ps[0:16, 2 * s:2 * s + 2, 0:HALF], ACT.Identity, bias=col("dtb")[0:16]).then_inc(acc_free[s], 1)
        act.activation(sp1[:, 0:1], col("alog")[0:16], ACT.Exp).then_inc(s_dta.sem, 1)
        split_hi(act, U_DT + R)
        act.wait_ge(s_dtd.sem, s_dtd.past("absneg"))
        act.activation(dty[:, :], dty[:, :], ACT.Exp)
        act.drain()
        act.activation(dty[:, :], dty[:, :], ACT.Ln, bias=1.0).then_inc(s_dta.sem, 1)
        act.wait_ge(s_cz, 1)

        def x_body(i):
            for j in range(4):
                m = i * 4 + j
                s, rnd = slot(U_XBC + j, i, 1)
                act.wait_ge(unit_done[s], rnd + 2)
                act.wait_ge(s_conv.sem, s_conv.past("conv", m, 2))
                act.activation(flat(cin[:, j % 2, 3:3 + TM], TM), acc(s, TM), ACT.Copy).then_inc(acc_free[s], 1)
                split_hi(act, U_XBC + j + R, i, 1)
                act.wait_ge(s_conv.sem, s_conv.past("conv", m))
                act.activation(xbc[:, m, FRONT:], cac[:, j % 2], ACT.Silu).then_inc(s_xbc.sem, 1)
        loop(act, 3, x_body)

        def z_body(i):
            for j in range(4):
                s, rnd = slot(U_Z + j, i, 1)
                act.wait_ge(unit_done[s], rnd + 2)
                act.activation(zs[:, i * 4 + j], acc(s, SEQ), ACT.Silu).then_inc(acc_free[s], 1)
                split_hi(act, U_Z + j + R, i, 1)
        loop(act, 2, z_body)

    def proj_dve(dve):
        dve.memset(xbc[:, :, 0:FRONT], 0.0)
        dve.memset(ad[:, 1, 0:FRONT], 0.0)
        dve.wait_ge(s_dta.sem, s_dta.past("exp"))
        dve.wait_ge(acc_free[U_DT % R], U_DT // R + 2)
        dve.tensor_scalar(dty[:, :], dtx[:, :], -1.0, None, ALU.mult)
        dve.tensor_scalar(sp1[:, 0:1], sp1[:, 0:1], -1.0, None, ALU.mult)
        dve.memset(cin[:, :, 0:3], 0.0).then_inc(s_cz, 1)
        dve.drain()
        dve.tensor_tensor(dty[:, :], dty[:, :], dtx[:, :], ALU.min).then_inc(s_dtd.sem, 1)
        dve.wait_ge(s_dta.sem, s_dta.past("ln"))
        dve.scalar_tensor_tensor(ad[:, 1, FRONT:], dtx[:, :], 0.0, dty[:, :], ALU.max, ALU.add)
        dve.drain()
        dve.tensor_scalar(ad[:, 0], ad[:, 1], sp1[:, 0:1], None, ALU.mult)
        dve.drain()
        dve.tensor_tensor_scan(ad[:, 0], keep, ad[:, 0], 0.0, ALU.mult, ALU.add).then_inc(s_dtd.sem, 1)

        def body(i):
            for j in range(4):
                m = i * 4 + j
                dve.wait_ge(acc_free[(U_XBC + j) % R], read_out(U_XBC + j, i, 1))
                dve.wait_ge(s_xbc.sem, s_xbc.past("x", m, 2))
                o = cac[:, j % 2]
                dve.tensor_scalar(o, cin[:, j % 2, 0:TM], col("cw0", m), col("cb", m), ALU.mult, ALU.add)
                for k in range(1, 4):
                    dve.drain()
                    ins = dve.scalar_tensor_tensor(o, cin[:, j % 2, k:k + TM], col(f"cw{k}", m), o, ALU.mult, ALU.add)
                ins.then_inc(s_conv.sem, 1)
                dve.drain()
        loop(dve, 3, body)

    s_cs = sem("silu_c")

    ZA1, ZA2 = O_HC + 40704, O_KC + 7168
    ar = [at(f"ar{h}", [P, 256], z) for h, z in enumerate((ZA1, ZA2))]

    def ada_pe(pe, i, part):
        for j in range(R):
            g = U_ADA + 4 * part + j
            s, rnd = slot(g, i, 3)
            pe.wait_ge(landed[s], (rnd + 1) * 16)
            w = wraw[:, s].rearrange("p (k a) m -> p k (a m)", k=2)
            for k in range(2):
                last = pe.matmul(ps[32 * part:32 * part + 2, 3, :], cs[:, 2 * j + k], w[:, k],
                                 start=j + k == 0, stop=j == R - 1 and k == 1)
            last.then_inc(lo_done[s], 1)

    def ada_act(act, i):
        for part in range(3):
            h = slice(32 * part, 32 * part + 2)
            s, rnd = slot(U_ADA + 4 * part + 3, i, 3)
            act.wait_ge(lo_done[s], rnd + 1)
            act.activation(ar[0][h], ps[h, 3, 0:256], ACT.Copy)
            ins = act.activation(ar[1][h], ps[h, 3, 256:512], ACT.Copy)
        ins.then_inc(f_a.sem, 1)
        act.wait_ge(f_p.sem, f_p.past("cols", i))
        cols = ps[:, 3, :].rearrange("p (j a c) -> p a j c", j=4, a=4)[:, 0:3, :, 0:2]
        act.activation(mod[:, :].rearrange("p l m c -> p (l m c)")[:, bass.ds(i * 24, 24)].rearrange("p (a j c) -> p a j c", a=3, j=4),
                       cols, ACT.Copy).then_inc(f_a.sem, 1)

    def ada_turn(pe, i):
        pe.wait_ge(f_a.sem, f_a.past("rows", i))
        for j in range(4):
            last = pe.transpose(ps[:, 3, j * P:(j + 1) * P], ar[j // 2][:, (j % 2) * P:(j % 2 + 1) * P], ident)
        last.then_inc(f_p.sem, 1)

    def ada_dve(dve):
        dve.wait_ge(f_a.sem, f_a.past("ada", NT - 1))
        for l in range(2):
            b = colr(f"bada{l}", 48).unsqueeze(2).to_broadcast([P, 48, 2])
            dve.tensor_tensor(mod[:, l], mod[:, l], b, ALU.add)
        dve.drain()
        for l in range(2):
            for k, off in ((0, 8), (1, 32)):
                g = colr(f"n{k + 1}{l}", 8).unsqueeze(2).to_broadcast([P, 8, 2])
                dve.tensor_scalar(gm[:, l, k], mod[:, l, off:off + 8], 1.0, None, ALU.add)
                dve.drain()
                dve.tensor_tensor(gm[:, l, k], gm[:, l, k], g, ALU.mult)
        dve.drain()

    Y = at("Y", [P, NT, NCH * CHUNK], O_HC)
    XS = O_X + 12288
    xc = at("xc", [P, XBC_TILES, CHUNK], XS)
    xdt = at("xdt", [P, 16, HEAD], XS + 6144)
    xe = at("xe", [P, 16, HEAD], XS + 10240)
    btok = at("btok", [P, 2, STATE], XS + 14336)
    cbm = at("cbm", [P, 2, CHUNK], XS + 15360)
    st = at("st", [P, 16, HEAD], XS + 16384)
    wd = at("wd", [P, 16, CHUNK], O_H)
    ce = at("ce", [P, 16, CHUNK], O_H + 8 * K)
    eb = at("eb", [P, 16, CHUNK], O_HH)
    d_v = steps("ssd_vector", "xc", "bt", "xdt", "dl", "xe", "wm", "yo", "state")
    d_p = steps("ssd_tensor", "xt", "bt", "bc", "y", "st")
    d_a = steps("ssd_scalar", "e", "w", "dte")
    d_g = steps("ssd_gpsimd", "ce")
    bc = ps[:, 4:8].rearrange("p a (h l) -> p (a h) l", h=4)

    def ssd_pe(pe):
        all_freed(pe, U_OUT1)

        def body(c):
            pe.wait_ge(d_v.sem, d_v.past("xc", c))
            pe.wait_ge(d_v.sem, d_v.past("state", c, 1))
            for m in range(8):
                last = pe.transpose(ps[:, m // 4, (m % 4) * P:(m % 4 + 1) * P], xc[:, m], ident)
            last.then_inc(d_p.sem, 1)
            for g in range(2):
                pe.transpose(ps[:, 2, g * P:(g + 1) * P], xc[:, 8 + g], ident)
            for k in range(2):
                pe.transpose(ps[:, 2, 256 + 16 * k:272 + 16 * k], ads[:, k], ident[0:16, 0:16])
            for g in range(2):
                last = pe.matmul(ps[:, 3, g * P:(g + 1) * P], xc[:, 8 + g], xc[:, 10 + g], start=True, stop=True)
            last.then_inc(d_p.sem, 1)
            for h in range(16):
                last = pe.matmul(bc[:, h], ident[0:16, h:h + 1].to_broadcast([16, P]), ads[:, 0], start=True, stop=True)
            last.then_inc(d_p.sem, 1)
            pe.wait_ge(d_v.sem, d_v.past("wm", c))
            pe.wait_ge(d_g.sem, d_g.past("ce", c))
            for h in range(16):
                o = ps[64 * (h % 2):64 * (h % 2) + 64, h // 8, (h // 2 % 4) * P:(h // 2 % 4 + 1) * P]
                pe.matmul(o, xdt[:, h], wd[:, h], start=True, stop=False)
                last = pe.matmul(o, st[:, h], ce[:, h], start=False, stop=True)
            last.then_inc(d_p.sem, 1)
            for g in range(2):
                last = pe.matmul(ps[:, 2 + g], btok[:, g], xe[:, 8 * g:8 * g + 8].rearrange("p a b -> p (a b)"),
                                 start=True, stop=True)
            last.then_inc(d_p.sem, 1)
        loop(pe, NCH, body)

    def ssd_act(act):
        def body(c):
            act.wait_ge(d_p.sem, d_p.past("bc", c))
            act.wait_ge(d_v.sem, d_v.past("state", c, 1))
            act.activation(eb[:, :], bc, ACT.Exp).then_inc(d_a.sem, 1)
            act.wait_ge(d_v.sem, d_v.past("dl", c))
            act.activation(wd[:, :], wd[:, :], ACT.Exp).then_inc(d_a.sem, 1)
            act.activation(dte[:, :], dte[:, :], ACT.Exp).then_inc(d_a.sem, 1)
        loop(act, NCH, body)

    def ssd_pool(pool):
        def body(c):
            pool.wait_ge(d_a.sem, d_a.past("e", c))
            pool.wait_ge(d_v.sem, d_v.past("xc", c))
            pool.wait_ge(d_p.sem, d_p.past("y", c, 1))
            for g in range(2):
                h = slice(8 * g, 8 * g + 8)
                ins = pool.tensor_tensor(ce[:, h], eb[:, h], xc[:, 10 + g].unsqueeze(1).to_broadcast([P, 8, CHUNK]), ALU.mult)
            ins.then_inc(d_g.sem, 1)
        loop(pool, NCH, body)

    def ssd_dve(dve):
        s, rnd = slot(U_Z + 7)
        dve.wait_ge(unit_done[s], rnd + 2)
        dve.memset(st[:, :], 0.0)
        dve.wait_ge(s_xbc.sem, s_xbc.past("x", XBC_TILES - 1))

        def body(c):
            t = bass.ds(c * CHUNK, CHUNK)
            dve.wait_ge(d_p.sem, d_p.past("y", c, 1))
            dve.wait_ge(d_g.sem, d_g.past("ce", c, 1))
            dve.tensor_copy(ads[:, :], ad[:, :, t])
            dve.tensor_copy(xc[:, :], xbc[:, :, t]).then_inc(d_v.sem, 1)
            dve.drain()
            dve.wait_ge(d_p.sem, d_p.past("bt", c))
            dve.wait_ge(d_p.sem, d_p.past("st", c, 1))
            dve.tensor_copy(adt[:, :], ps[:, 2, 256:288].rearrange("p (a b) -> p a b", a=2))
            dve.tensor_copy(btok[:, :], ps[:, 2, 0:256].rearrange("p (a b) -> p a b", a=2))
            dve.tensor_tensor(cbm[:, :], ps[:, 3, 0:256].rearrange("p (a b) -> p a b", a=2),
                                      tri.unsqueeze(1).to_broadcast([P, 2, CHUNK]), ALU.mult).then_inc(d_v.sem, 1)
            dve.drain()
            dve.tensor_tensor(xdt[:, :], ps[:, 0:2].rearrange("p a (h d) -> p (a h) d", d=HEAD),
                                      adt[:, 1].unsqueeze(2).to_broadcast([P, 16, HEAD]), ALU.mult).then_inc(d_v.sem, 1)
            dve.drain()
            dve.wait_ge(d_a.sem, d_a.past("e", c))
            for h in range(16):
                dve.tensor_scalar(wd[:, h], bc[:, h], adt[:, 0, h:h + 1], 0.0, ALU.subtract, ALU.min)
            dve.tensor_tensor(dte[:, :], bc[:, :, CHUNK - 1], adt[:, 0], ALU.subtract).then_inc(d_v.sem, 1)
            dve.wait_ge(d_a.sem, d_a.past("dte", c))
            dve.tensor_tensor(xe[:, :], xdt[:, :], dte[:, :].unsqueeze(2).to_broadcast([P, 16, HEAD]), ALU.mult).then_inc(d_v.sem, 1)
            for g in range(2):
                h = slice(8 * g, 8 * g + 8)
                ins = dve.tensor_tensor(wd[:, h], wd[:, h], cbm[:, g].unsqueeze(1).to_broadcast([P, 8, CHUNK]), ALU.mult)
            ins.then_inc(d_v.sem, 1)
            dve.wait_ge(d_p.sem, d_p.past("y", c))
            for m in range(8):
                ins = dve.scalar_tensor_tensor(Y[:, m, t], xc[:, m], col("dskip", m),
                                               ps[:, m // 4, (m % 4) * P:(m % 4 + 1) * P], ALU.mult, ALU.add)
            ins.then_inc(d_v.sem, 1)
            dve.drain()
            dve.tensor_tensor(st[:, :], st[:, :], eb[:, :, CHUNK - 1:].to_broadcast([P, 16, HEAD]), ALU.mult)
            dve.drain()
            dve.wait_ge(d_p.sem, d_p.past("st", c))
            dve.tensor_tensor(st[:, :], st[:, :], ps[:, 2:4].rearrange("p a (h d) -> p (a h) d", d=HEAD), ALU.add).then_inc(d_v.sem, 1)
            dve.drain()
        loop(dve, NCH, body)
        all_freed(dve, U_OUT1)
        dve.tensor_tensor(Y[:, :, CHUNK:], Y[:, :, CHUNK:], zs[:, :], ALU.mult).then_inc(s_yg.sem, 1)
        dve.drain()

    s_yg = steps("ssd_gated", "gated")
    ysrc = lambda kt: Y[:, kt, CHUNK:]

    def add_pe(pe, U, n, xh, xl, T, nk=8, ready=None):
        if ready is not None:
            for kt in range(nk):
                ready(kt)
        loop(pe, n, lambda i: [pe_unit(pe, U + j, i, 1, xh, xl, T, nk) for j in range(4)])

    def add_dve(dve, U, n, dst, T, gate=None):
        def body(i):
            for j in range(4):
                s, rnd = slot(U + j, i, 1)
                dve.wait_ge(unit_done[s], rnd + 2)
                m = i * 4 + j
                d = dst[:, m, 0:T]
                if gate is None:
                    ins = dve.tensor_tensor(d, d, ps[:, s, 0:T], ALU.add)
                else:
                    ins = dve.scalar_tensor_tensor(d, ps[:, s, 0:T], gate(m), d, ALU.mult, ALU.add)
                ins.then_inc(acc_free[s], 1)
        loop(dve, n, body)
        dve.drain()

    Z1, Z2, ZB = O_HC, SC + 4 * NT * TM, O_KC
    ej = at("ej", [P, 2, NPAIR, NB], Z1)
    cab = at("cab", [P, 2, 4, 2, 9, 16], Z1 + 16896)
    ba = at("ba", [P, 2, 4, LB, 16], Z1 + 26112)
    bat = at("bat", [P, 2, 4, P], Z1 + 30208)
    mt = at("mt", [P, 8, P], Z1 + 34304)
    pw = at("pw", [P, 2, 9, NPAIR], Z1 + 38400)
    bbar = at("bbar", [P, 2, NPAIR, 16], ZB)
    pm = at("pm", [P, 24, NPAIR], ZB + 4096)
    us = at("us", [P, TM], Z2)
    u2 = at("u2", [P, 8, LB, 16], Z2 + 2112)
    u3 = at("u3", [P, 8, NB], Z2 + 6208)
    spv = at("spv", [P, 2, 4, NB], Z2 + 8320)
    dec = at("dec", [P, 4, NB], Z2 + 10432)
    vv = at("vv", [P, 2, 4, NB], Z2 + 11488)
    sv = at("sv", [P, 2, 4, NB], Z2 + 13600)
    t1 = at("t1", [P, 576], Z2 + 15712)
    t2 = at("t2", [P, 576], Z2 + 18016)
    ka = at("ka", [16, 8, LB, 16], Z2 + 20320)
    bc5 = at("bc5", [P, 4, NPAIR, 16], Z2 + 24416)
    d5 = at("d5", [16, S5_G], Z2 + 32608)
    dd = at("dd", [16, 8, 16], Z2 + 32864)
    yg = at("yg", [P, SEQ], Z2 + 11488)
    y2 = at("y2", [P, LB, 8, 16], Z2 + 2112)
    assert Z2 + 33376 + base <= 229368

    s_5in = sem("s5_inputs")
    e_pa, e_pv = steps("s5_param_scalar", "step", "mag", "sin"), steps("s5_param_vector", "ls", "angle", "done")
    f_v = steps("s5_vector", "ba", "u2s", "ka", "rot", "sp", "y2s", "lo")
    f_p = steps("s5_tensor", "u2", "bat", "k", "u3", "w", "y", "yt", "cols")
    f_a = steps("s5_scalar", "us", "bat", "u3", "g", "hi", "rows", "ada")
    f_d = sem("s5_kernel_moved")
    s_m0 = sem("s5_zeroed")
    LR, LI, LS, X1, X8, TH, NN, RR, CN, SN, MG, M8, DEN, AM, CR, CI, Q1, Q2 = range(18)
    E8 = 18

    def q(k):
        return pm[:, k]

    def tt(dve, o, a, b, op):
        dve.tensor_tensor(o, a, b, op)
        dve.drain()

    def cmul(dve, o_re, o_im, a, b, ta, tb):
        tt(dve, ta, a[0], b[0], ALU.mult)
        tt(dve, tb, a[1], b[1], ALU.mult)
        tt(dve, o_re, ta, tb, ALU.subtract)
        tt(dve, ta, a[0], b[1], ALU.mult)
        tt(dve, tb, a[1], b[0], ALU.mult)
        tt(dve, o_im, ta, tb, ALU.add)

    def s5_param_act(act):
        act.wait_ge(s_5in, 48)
        act.wait_ge(s_yg.sem, s_yg.past("gated"))
        act.activation(q(LS), q(LS), ACT.Exp).then_inc(e_pa.sem, 1)
        act.wait_ge(e_pv.sem, e_pv.past("ls"))
        act.activation(q(MG), q(X1), ACT.Exp)
        act.activation(q(M8), q(X1), ACT.Exp, scale=8.0).then_inc(e_pa.sem, 1)
        act.wait_ge(e_pv.sem, e_pv.past("angle"))
        act.activation(q(SN), q(RR), ACT.Sin)
        act.activation(q(CN), q(Q1), ACT.Sin, bias=col("halfpi"), scale=-1.0).then_inc(e_pa.sem, 1)

    def s5_param_dve(dve):
        dve.wait_ge(s_5in, 48)
        s, rnd = slot(U_OUT1 + 7)
        dve.wait_ge(unit_done[s], rnd + 2)
        dve.memset(cab[:, :], 0.0)
        dve.memset(ar[0][:, :], 0.0)
        dve.memset(ar[1][:, :], 0.0)
        dve.memset(spv[:, :, :, 0:1], 0.0)
        dve.memset(mt[:, :], 0.0).then_inc(s_m0, 1)
        dve.wait_ge(e_pa.sem, e_pa.past("step"))
        tt(dve, q(X1), q(LR), q(LS), ALU.mult)
        dve.tensor_tensor(q(TH), q(LI), q(LS), ALU.mult).then_inc(e_pv.sem, 1)
        dve.drain()
        dve.tensor_scalar(q(NN), q(TH), 1.0 / (2 * math.pi), ROUND, ALU.mult, ALU.add)
        dve.drain()
        dve.tensor_scalar(q(NN), q(NN), ROUND, None, ALU.subtract)
        dve.drain()
        dve.scalar_tensor_tensor(q(RR), q(NN), -TWO_PI_HI, q(TH), ALU.mult, ALU.add)
        dve.drain()
        dve.scalar_tensor_tensor(q(RR), q(NN), -TWO_PI_LO, q(RR), ALU.mult, ALU.add)
        dve.drain()
        dve.tensor_scalar(q(RR), q(RR), 3.1415925, -3.1415925, ALU.min, ALU.max)
        dve.drain()
        dve.scalar_tensor_tensor(q(Q1), q(RR), -1.0, q(RR), ALU.mult, ALU.max).then_inc(e_pv.sem, 1)
        dve.memset(pw[:, 0, 0], 1.0)
        dve.memset(pw[:, 1, 0], 0.0)
        dve.memset(ej[:, 0, :, 0:1], 1.0)
        dve.memset(ej[:, 1, :, 0:1], 0.0)
        dve.wait_ge(e_pa.sem, e_pa.past("sin"))
        tt(dve, pw[:, 0, 1], q(MG), q(CN), ALU.mult)
        tt(dve, pw[:, 1, 1], q(MG), q(SN), ALU.mult)
        tt(dve, q(Q1), q(LR), q(LR), ALU.mult)
        tt(dve, q(Q2), q(LI), q(LI), ALU.mult)
        tt(dve, q(DEN), q(Q1), q(Q2), ALU.add)
        dve.reciprocal(q(DEN), q(DEN))
        dve.tensor_scalar(q(AM), pw[:, 0, 1], -1.0, None, ALU.add)
        dve.drain()
        tt(dve, q(Q1), q(AM), q(LR), ALU.mult)
        tt(dve, q(Q2), pw[:, 1, 1], q(LI), ALU.mult)
        tt(dve, q(CR), q(Q1), q(Q2), ALU.add)
        tt(dve, q(Q1), pw[:, 1, 1], q(LR), ALU.mult)
        tt(dve, q(Q2), q(AM), q(LI), ALU.mult)
        tt(dve, q(CI), q(Q1), q(Q2), ALU.subtract)
        tt(dve, q(CR), q(CR), q(DEN), ALU.mult)
        tt(dve, q(CI), q(CI), q(DEN), ALU.mult)
        ta, tb = (t[:, 0:512].rearrange("p (a b) -> p a b", a=NPAIR) for t in (t1, t2))
        wide = lambda x: x.unsqueeze(2).to_broadcast([P, NPAIR, 16])
        cmul(dve, bbar[:, 0], bbar[:, 1], (bc5[:, 0], bc5[:, 1]), (wide(q(CR)), wide(q(CI))), ta, tb)
        for a, n in ((1, 1), (2, 2), (4, 4)):
            ta, tb = (t[:, 0:n * NPAIR].rearrange("p (a b) -> p a b", a=n) for t in (t1, t2))
            b = tuple(pw[:, r, a].unsqueeze(1).to_broadcast([P, n, NPAIR]) for r in range(2))
            cmul(dve, pw[:, 0, a + 1:a + 1 + n], pw[:, 1, a + 1:a + 1 + n],
                 (pw[:, 0, 1:1 + n], pw[:, 1, 1:1 + n]), b, ta, tb)
        for k in range(3):
            src = (q(CN), q(SN)) if k == 0 else (q(E8), q(E8 + 1))
            cmul(dve, q(E8 + 2), q(E8 + 3), src, src, q(Q1), q(Q2))
            dve.tensor_copy(pm[:, E8:E8 + 2], pm[:, E8 + 2:E8 + 4])
            dve.drain()
        n = 1
        while n < NB:
            m = min(n, NB - n)
            for c0 in range(0, m, 16):
                w = min(16, m - c0)
                ta, tb = (t[:, 0:NPAIR * w].rearrange("p (a b) -> p a b", a=NPAIR) for t in (t1, t2))
                b = tuple(q(E8 + r).unsqueeze(2).to_broadcast([P, NPAIR, w]) for r in range(2))
                cmul(dve, ej[:, 0, :, n + c0:n + c0 + w], ej[:, 1, :, n + c0:n + c0 + w],
                     (ej[:, 0, :, c0:c0 + w], ej[:, 1, :, c0:c0 + w]), b, ta, tb)
            cmul(dve, q(E8 + 2), q(E8 + 3), (q(E8), q(E8 + 1)), (q(E8), q(E8 + 1)), q(Q1), q(Q2))
            dve.tensor_copy(pm[:, E8:E8 + 2], pm[:, E8 + 2:E8 + 4])
            dve.drain()
            n *= 2

    def s5_dve(dve):
        def body(i):
            pr = bass.ds(i * 4, 4)
            dve.drain()
            dve.wait_ge(f_p.sem, f_p.past("yt", i, 1))
            dve.wait_ge(f_a.sem, f_a.past("hi", i, 1))
            ta, tb = (t[:, 0:512].rearrange("p (q k h) -> p q k h", q=4, k=8) for t in (t1, t2))
            pk = tuple(pw[:, r, 0:8, pr].rearrange("p k q -> p q k").unsqueeze(3).to_broadcast([P, 4, 8, 16]) for r in range(2))
            bb = tuple(bbar[:, r, pr].unsqueeze(2).to_broadcast([P, 4, 8, 16]) for r in range(2))
            cmul(dve, ba[:, 0], ba[:, 1], bb, pk, ta, tb)
            ta, tb = (t[:, 0:576].rearrange("p (q k h) -> p q k h", q=4, k=9) for t in (t1, t2))
            pk = tuple(pw[:, r, 0:9, pr].rearrange("p k q -> p q k").unsqueeze(3).to_broadcast([P, 4, 9, 16]) for r in range(2))
            cc = tuple(bc5[:, 2 + r, pr].unsqueeze(2).to_broadcast([P, 4, 9, 16]) for r in range(2))
            tt(dve, ta, cc[0], pk[0], ALU.mult)
            tt(dve, tb, cc[1], pk[1], ALU.mult)
            for g in range(2):
                h = slice(64 * g, 64 * g + 64)
                dve.tensor_tensor(cab[h, 0, :, g].rearrange("p q k h -> p q (k h)"), ta[h].rearrange("p q k h -> p q (k h)"), tb[h].rearrange("p q k h -> p q (k h)"), ALU.subtract)
            dve.drain()
            tt(dve, ta, cc[0], pk[1], ALU.mult)
            tt(dve, tb, cc[1], pk[0], ALU.mult)
            for g in range(2):
                h = slice(64 * g, 64 * g + 64)
                ins = dve.scalar_tensor_tensor(cab[h, 1, :, g].rearrange("p q k h -> p q (k h)"), ta[h].rearrange("p q k h -> p q (k h)"),
                                               -1.0, tb[h].rearrange("p q k h -> p q (k h)"), ALU.mult, ALU.subtract)
            ins.then_inc(f_v.sem, 1)
            dve.drain()
            dve.wait_ge(f_p.sem, f_p.past("u2", i))
            dve.tensor_copy(u2[0:NB].rearrange("p g k h -> p k g h"),
                                    ps[0:NB, 4:6].rearrange("p a (k g h) -> p (a k) g h", k=4, g=8)).then_inc(f_v.sem, 1)
            dve.wait_ge(f_p.sem, f_p.past("k", i))
            dve.wait_ge(f_d, (i + 1) * 128)
            dve.tensor_tensor(dd[:, :], ident[0:16, 0:16].unsqueeze(1).to_broadcast([16, 8, 16]),
                              d5[:, bass.ds(i * 8, 8)].unsqueeze(2).to_broadcast([16, 8, 16]), ALU.mult)
            dve.tensor_copy(ka[:, :], ps[0:16, 2:4].rearrange("p a (g k h) -> p (a g) k h", g=4, k=8))
            dve.drain()
            dve.tensor_tensor(ka[:, :, 0], ka[:, :, 0], dd[:, :], ALU.add).then_inc(f_v.sem, 1)
            dve.drain()
            dve.tensor_copy(dec[:, :, 1:], pm[:, M8, pr].unsqueeze(2).to_broadcast([P, 4, NB - 1]))
            dve.memset(dec[:, :, 0:1], 0.0)
            dve.wait_ge(f_p.sem, f_p.past("w", i))
            er, ei = ej[:, 0, pr], ej[:, 1, pr]
            wr, wi = (ps[:, b, 0:4 * NB].rearrange("p (q c) -> p q c", q=4) for b in (4, 5))
            ta, tb, tc, td = (t[:, o:o + 4 * NB].rearrange("p (q c) -> p q c", q=4) for t in (t1, t2) for o in (0, 288))
            dve.tensor_tensor(ta, wr, er, ALU.mult)
            dve.tensor_tensor(tb, wi, ei, ALU.mult)
            dve.tensor_tensor(tc, wi, er, ALU.mult)
            dve.tensor_tensor(td, wr, ei, ALU.mult).then_inc(f_v.sem, 1)
            dve.drain()
            dve.tensor_tensor(vv[:, 0], ta, tb, ALU.add)
            dve.tensor_tensor(vv[:, 1], tc, td, ALU.subtract)
            dve.drain()
            dm = dec[:, :].rearrange("p q c -> p (q c)")
            for r in range(2):
                dve.tensor_tensor_scan(sv[:, r].rearrange("p q c -> p (q c)"), dm, vv[:, r].rearrange("p q c -> p (q c)"), 0.0, ALU.mult, ALU.add)
            dve.drain()
            dve.tensor_tensor(ta, sv[:, 0], er, ALU.mult)
            dve.tensor_tensor(tb, sv[:, 1], ei, ALU.mult)
            dve.tensor_tensor(tc, sv[:, 0], ei, ALU.mult)
            dve.tensor_tensor(td, sv[:, 1], er, ALU.mult)
            dve.drain()
            n = NB - 1
            dve.tensor_tensor(spv[:, 0, :, 1:], ta[:, :, 0:n], tb[:, :, 0:n], ALU.subtract)
            dve.tensor_tensor(spv[:, 1, :, 1:], tc[:, :, 0:n], td[:, :, 0:n], ALU.add).then_inc(f_v.sem, 1)
            dve.drain()
            dve.wait_ge(f_p.sem, f_p.past("y", i))
            dve.tensor_copy(y2[0:NB].rearrange("p k g h -> p g k h"),
                                    ps[0:NB, 6:8].rearrange("p a (g k h) -> p (a g) k h", g=4, k=8)).then_inc(f_v.sem, 1)
            dve.wait_ge(f_a.sem, f_a.past("hi", i))
            dve.tensor_tensor(hlo[:, i], yg[:, :], hhi[:, i].bitcast(F32), ALU.subtract).then_inc(f_v.sem, 1)
            dve.drain()
        loop(dve, NT, body)

    def s5_pe(pe):
        pe.wait_ge(s_m0, 1)
        all_freed(pe, U_GLU)

        def body(i):
            pe.wait_ge(f_a.sem, f_a.past("us", i))
            pe.wait_ge(f_v.sem, f_v.past("rot", i, 1))
            for k in range(LB):
                kk = LB - 1 - k
                last = pe.transpose(ps[0:NB, 4 + kk // 4, (kk % 4) * P:(kk % 4 + 1) * P], us[:, k::LB], ident)
            last.then_inc(f_p.sem, 1)
            pe.wait_ge(f_v.sem, f_v.past("ba", i))
            pe.wait_ge(f_a.sem, f_a.past("g", i, 1))
            for r in range(2):
                for p in range(4):
                    last = pe.transpose(ps[:, r, p * P:(p + 1) * P], ba[:, r, p].rearrange("p k h -> p (k h)"), ident)
            last.then_inc(f_p.sem, 1)
            pe.wait_ge(f_v.sem, f_v.past("ka", i, 1))
            pe.wait_ge(f_a.sem, f_a.past("ada", i, 1))
            for p in range(4):
                o = ps[0:16, 2 + p // 2, (p % 2) * 256:(p % 2 + 1) * 256]
                for r in range(2):
                    last = pe.matmul(o, ba[:, r, p, 0], cab[:, r, p, :, 0:8].rearrange("p g k h -> p g (k h)"),
                                     start=r == 0, stop=r == 1)
            last.then_inc(f_p.sem, 1)
            pe.wait_ge(f_v.sem, f_v.past("u2s", i))
            pe.wait_ge(f_v.sem, f_v.past("y2s", i, 1))
            for g in range(8):
                last = pe.transpose(ps[:, 6 + g // 4, (g % 4) * NB:(g % 4 + 1) * NB],
                                    u2[0:NB, g].rearrange("p k h -> p (k h)"), ident[0:NB, 0:NB])
            last.then_inc(f_p.sem, 1)
            pe.wait_ge(f_a.sem, f_a.past("u3", i))
            for p in range(4):
                for r in range(2):
                    for g in range(2):
                        last = pe.matmul(ps[64 * g:64 * g + 64, 4 + r, p * NB:(p + 1) * NB],
                                         bat[:, r, p, 64 * g:64 * g + 64], u3[:, 2 * p + g], start=True, stop=True)
            last.then_inc(f_p.sem, 1)
            pe.wait_ge(f_v.sem, f_v.past("ka", i))
            ada_pe(pe, i, 0)
            pe.wait_ge(f_v.sem, f_v.past("sp", i))
            pe.wait_ge(f_d, (i + 2) * 128)
            for p in range(4):
                o = ps[0:NB, 6 + p // 2, (p % 2) * 256:(p % 2 + 1) * 256]
                for r in range(2):
                    pe.matmul(o, spv[:, r, p], cab[:, r, p, :, 1:9].rearrange("p g k h -> p g (k h)"), start=r == 0, stop=False)
                for g in range(2):
                    last = pe.matmul(o[:, g * P:(g + 1) * P], u3[:, 2 * p + g], mt[:, 2 * p + g], start=False, stop=g == 1)
            last.then_inc(f_p.sem, 1)
            ada_pe(pe, i, 1)
            pe.wait_ge(f_v.sem, f_v.past("y2s", i))
            for k in range(LB):
                last = pe.transpose(ps[:, k // 4, (k % 4) * NB:(k % 4 + 1) * NB],
                                    y2[0:NB, k].rearrange("p g h -> p (g h)"), ident[0:NB, 0:NB])
            last.then_inc(f_p.sem, 1)
            ada_pe(pe, i, 2)
            ada_turn(pe, i)
        loop(pe, NT, body)

    def s5_act(act):
        act.wait_ge(s_m0, 1)

        def body(i):
            act.wait_ge(f_p.sem, f_p.past("u2", i, 1))
            act.activation(us[:, :], uT[:, i], ACT.Copy).then_inc(f_a.sem, 1)
            act.wait_ge(f_p.sem, f_p.past("bat", i))
            act.activation(bat[:, :], ps[:, 0:2].rearrange("p r (q m) -> p r q m", q=4), ACT.Copy).then_inc(f_a.sem, 1)
            act.wait_ge(f_p.sem, f_p.past("u3", i))
            act.wait_ge(f_p.sem, f_p.past("y", i, 1))
            act.activation(u3[:, :].rearrange("p (a g) c -> p a (g c)", a=2),
                                   ps[:, 6:8, 0:4 * NB], ACT.Copy).then_inc(f_a.sem, 1)
            act.wait_ge(f_v.sem, f_v.past("ka", i))
            act.wait_ge(f_p.sem, f_p.past("y", i, 1))
            for k in range(LB):
                r0 = 16 * (LB - 1 - k)
                act.dma_start(mt[r0:r0 + 16, :, 16 * k:], ka[:, :, 0:LB - k].rearrange("p g k h -> p g (k h)")).then_inc(f_d, 16)
            act.wait_ge(f_p.sem, f_p.past("yt", i))
            act.wait_ge(f_v.sem, f_v.past("lo", i, 1))
            for b in range(2):
                ins = act.activation(yg[:, :].rearrange("p (c k) -> p k c", k=LB)[:, 4 * b:4 * b + 4],
                                     ps[:, b, 0:4 * NB].rearrange("p (k c) -> p k c", k=4)[:, :, NB0:], ACT.Gelu)
            ins.then_inc(f_a.sem, 1)
            act.drain()
            act.activation(hhi[:, i], yg[:, :], ACT.Copy).then_inc(f_a.sem, 1)
            ada_act(act, i)
        loop(act, NT, body)

    def s5_ready(pe):
        return lambda kt: pe.wait_ge(f_v.sem, f_v.past("lo", kt))

    sgl = at("sgl", [P, 2, SEQ], SC + 16 * K)
    s5o = at("s5o", [P, NT, SEQ], SC)

    def pairs_pe(pe, U, n, xh, xl, T):
        loop(pe, n, lambda i: [pe_unit(pe, U + j, i, 1, xh, xl, T) for j in range(4)])

    def glu_act(act):
        act.wait_ge(f_v.sem, f_v.past("lo", NT - 1))

        def body(i):
            for j in range(2):
                split_hi(act, U_GLU + 2 * j + R, i, 1)
                s, rnd = slot(U_GLU + 2 * j + 1, i, 1)
                act.wait_ge(unit_done[s], rnd + 2)
                act.wait_ge(acc_free[(U_GLU + 2 * j) % R], read_out(U_GLU + 2 * j, i, 1, 1))
                act.activation(sgl[:, j], ps[:, s, :], ACT.Sigmoid, bias=col("b_glu", i * 2 + j + 8)).then_inc(acc_free[s], 1)
                split_hi(act, U_GLU + 2 * j + 1 + R, i, 1)
        loop(act, 4, body)

    def glu_dve(dve):
        def body(i):
            for j in range(2):
                s, rnd = slot(U_GLU + 2 * j, i, 1)
                dve.wait_ge(unit_done[s], rnd + 2)
                dve.wait_ge(acc_free[(U_GLU + 2 * j + 1) % R], read_out(U_GLU + 2 * j + 1, i, 1))
                ins = dve.scalar_tensor_tensor(s5o[:, i * 2 + j], ps[:, s, :], col("b_glu", i * 2 + j), sgl[:, j], ALU.add, ALU.mult)
                ins.then_inc(acc_free[s], 1)
            dve.drain()
        loop(dve, 4, body)

    rl = at("rl", [P, 2, SEQ], SC)
    m_v, m_h, m_l = steps("mlp_square", "v"), steps("mlp_hi", "hi"), steps("mlp_lo", "lo")
    rv = at("rv", [P, 2, SEQ], SC + 4 * K)

    def mlp_pe(pe):
        def chunk(c):
            for h in range(2):
                for j in range(4):
                    pe_unit(pe, U_FF + 4 * h + j, c, 4, xhi, xlo, SEQ)
            for h in range(2):
                for j in range(4):
                    ready = (lambda kt: pe.wait_ge(m_l.sem, m_l.past("lo", c * 8 + kt))) if h + j == 0 else None
                    pe_unit(pe, U_FF + 8 + 4 * h + j, c, 4, hhi, hlo, SEQ, ready=ready)
        for kt in range(NT):
            normed("mlp")(pe)(kt)
        loop(pe, 4, chunk)

    def mlp_act(act):
        act.wait_ge(n_hi.sem, n_hi.past("hi", hi_before[NORM["mlp"]] + NT - 1))

        def chunk(c):
            for m in range(8):
                s, rnd = slot(U_FF + m, c, 4)
                act.wait_ge(unit_done[s], rnd + 2)
                act.wait_ge(m_v.sem, m_v.past("v", c * 8 + m, 2))
                ins = act.activation(rl[:, m % 2], ps[:, s, :], ACT.Relu)
                ins.then_inc(acc_free[s], 1)
                split_hi(act, U_FF + m + R, c, 4)
                act.wait_ge(m_v.sem, m_v.past("v", c * 8 + m))
                act.activation(hhi[:, m], rv[:, m % 2], ACT.Copy).then_inc(m_h.sem, 1)
            for m in range(8):
                split_hi(act, U_FF + 8 + m + R, c, 4)
        loop(act, 4, chunk)

    def mlp_dve(dve):
        def chunk(c):
            for m in range(8):
                dve.wait_ge(acc_free[(U_FF + m) % R], read_out(U_FF + m, c, 4))
                dve.wait_ge(m_h.sem, m_h.past("hi", c * 8 + m, 2))
                dve.tensor_tensor(rv[:, m % 2], rl[:, m % 2], rl[:, m % 2], ALU.mult).then_inc(m_v.sem, 1)
                dve.wait_ge(m_h.sem, m_h.past("hi", c * 8 + m))
                dve.tensor_tensor(hlo[:, m], rv[:, m % 2], hhi[:, m].bitcast(F32), ALU.subtract).then_inc(m_l.sem, 1)
                if m % 2:
                    dve.drain()
            for m in range(8):
                s, rnd = slot(U_FF + 8 + m, c, 4)
                dve.wait_ge(unit_done[s], rnd + 2)
                ins = dve.tensor_tensor(res[:, m], res[:, m], ps[:, s, :], ALU.add)
                ins.then_inc(acc_free[s], 1)
            dve.drain()
        loop(dve, 4, chunk)

    qT = at("qT", [P, 4, SEQ], SC)
    kT = at("kT", [P, 4, 6 * P], SC + 8 * K)
    vT = at("vT", [P, 6, CONV], SC + 20 * K)
    pex = at("pex", [P, 2, SEQ], O_HH)
    pT = at("pT", [P, 2, SEQ], O_HH + 4 * K)
    ct = at("ct", [P, SEQ], O_HL + 14 * K)
    osb = at("osb", [P, 4, CONV], SC + 40 * K + 768)
    sm = at("sm", [P, 3, 4], SC + 48 * K + 768)
    biasb = at("biasb", [P, 2, 4, 2 * P], O_HH + 8 * K)
    qst = at("qst", [P, SEQ], O_HL + 8 * K)
    kst = at("kst", [P, 6 * P], O_HL + 10 * K)
    kcs = at("kcs", [P, CTX], O_HL + 13 * K)
    raw = at("raw", [P, 2, SEQ], O_HL + 8 * K)
    rt = at("rt", [P, 2, SEQ], O_HL + 12 * K)
    vraw = at("vraw", [P, 2, SEQ], O_HH + 8 * K)
    ub = at("ub", [P, 4, SEQ + 2 * PADT], SC + 32 * K)
    co = at("co", [P, 4, SEQ], O_HL)
    cn = at("cn", [P, 4, SEQ], SC + 32 * K)
    gs = at("gs", [P, 2, SEQ], O_HH + 8 * K)
    mhi = at("mhi", [P, NT, SEQ], SC, F32R)
    mlo = at("mlo", [P, NT, SEQ], SC + 16 * K, F32R)
    gt = at("gt", [P, 2 * NT, SEQ], SC)
    mv = at("mv", [P, 2, SEQ], SC + 40 * K)
    fa = at("fa", [P, 2, 2, SEQ], SC)
    fs = at("fs", [P, 2, 2, SEQ], SC + 8 * K)
    lsq = at("lsq", [P, 4, SEQ], SC + 40 * K)
    lmu = at("lmu", [P, SEQ], O_HH)
    lrs = at("lrs", [P, SEQ], O_HH + 2 * K)

    s_bias = sem("attn_bias_landed")
    shared = {}
    U_KV = N_B1 + 2 * N_LAYER

    class Pass:

        def __init__(self, key, layer, lat, U):
            self.key, self.l, self.lat, self.U = key, layer, lat, U
            self.bias0 = 64 * layer
            self.T = SEQ if lat else CTX
            self.res = res if lat else resc
            self.ci = 0 if lat else 1
            full, nu = self.U != U_KV, 4 * 2 * (4 if lat else 2)

            def s(name, *names, passes):
                if name not in shared:
                    shared[name] = steps(name, *names)
                return shared[name].part(passes if full or name[:3] in ("qk_", "v_r", "v_t", "v_d") else 0)

            nq = 8 if full else 4
            self.q_p = s("qk_rot", "rot", passes=nq if lat else 0)
            self.q_v = s("qk_done", "q", passes=nq)
            self.v_p, self.v_v = (
                s("v_turned", "t", passes=4), s("v_done", "v", passes=4))
            self.c_v = s("conv_v", "acc", "cen", "t", "lo", passes=1)
            self.c_a, self.c_p = s("conv_a", "sq", "root", "y", "hi", passes=1), s("conv_p", "mu", "var", passes=1)
            self.c_g = s("conv_taps", "conv", passes=POOL_TAPS - 1)
            self.c_lo = s("conv_lo", "lo", passes=1)
            self.a_st = s("attn_staged", "st", passes=4)
            self.a_s, self.a_max, self.a_exp, self.a_turn, self.a_pt, self.a_pv, self.a_out = (
                s(f"attn_{k}", k, passes=nu) for k in ("scores", "max", "exp", "turned", "copied", "values", "out"))
            self.o_p, self.o_a, self.o_v = (s(f"aout_{k}", k, passes=4) for k in ("t", "hi", "lo"))
            self.m_v, self.m_h = s("merge_v", "v", "lo", passes=8), s("merge_h", "hi", passes=8)
            self.f_a, self.f_v, self.f_h = (s("ffn_a", "a", "g", passes=22), s("ffn_v", "h", "lo", passes=22),
                                            s("ffn_s", "silu", "hi", passes=22))

        def src(self, kt):
            return self.res[:, kt, 0:self.T]

        def gain(self, k):
            return lambda kt: gm[:, self.l, k, kt, self.ci:self.ci + 1]

        def modv(self, part):
            return lambda kt: mod[:, self.l, bass.ds(part * 8 + kt, 1), self.ci]

        def norm(self, k):
            return NORM[f"{self.key}{'ab'[k]}"]

    def grid(ap):
        return ap.rearrange("p (r c) -> p c r", r=GH)

    def bycol(ap):
        return ap.rearrange("p (c r) -> p c r", r=GH)

    def inproj_pe(pe, p, glu=True):
        n0 = p.norm(0)
        for kt in range(NT):
            pe.wait_ge(n_lo.sem, n_lo.past("lo", hi_before[n0] + kt))
        if glu:
            loop(pe, 2, lambda i: [pe_unit(pe, p.U + j, i, 1, xhi, xlo, p.T) for j in range(4)])
        Uq, nq = (p.U + 8, 8) if glu else (p.U, 4)
        if glu:
            def qk(i):
                for j in range(4):
                    pe_unit(pe, Uq + j, i, 1, xhi, xlo, p.T)
                    if p.lat:
                        rotate(i, i * 4 + j, j)

            def rotate(i, m, j):
                pe.wait_ge(acc_free[(Uq + j) % R], read_out(Uq + j, i, 1))
                pe.wait_ge(p.q_v.sem, p.q_v.past("q", m, 2))
                pe.matmul(ps[:, 4 + j % 2, :], rot, raw[:, j % 2], start=True, stop=True).then_inc(p.q_p.sem, 1)
            loop(pe, 2, qk)
        else:
            for j in range(4):
                pe_unit(pe, Uq + j, 0, 0, xhi, xlo, p.T)
        Uv = Uq + nq
        for j in range(4):
            pe_unit(pe, Uv + j, 0, 0, xhi, xlo, p.T)
            pe.wait_ge(acc_free[(Uv + j) % R], read_out(Uv + j))
            if j >= 2:
                pe.wait_ge(p.v_v.sem, p.v_v.past("v", j - 2))
            for b in range(p.T // P):
                last = pe.transpose(ps[:, 6 + j % 2, b * P:(b + 1) * P], vraw[:, j % 2, b * P:(b + 1) * P], ident)
            last.then_inc(p.v_p.sem, 1)

    def inproj_act(act, p, glu=True):
        T = p.T
        if glu:
            def gb(i):
                for j in range(2):
                    m = i * 2 + j
                    split_hi(act, p.U + 2 * j + R, i, 1)
                    s, rnd = slot(p.U + 2 * j + 1, i, 1)
                    act.wait_ge(unit_done[s], rnd + 2)
                    act.wait_ge(acc_free[(p.U + 2 * j) % R], read_out(p.U + 2 * j, i, 1, 1))
                    act.activation(gs[:, j, 0:T], ps[:, s, 0:T], ACT.Sigmoid).then_inc(acc_free[s], 1)
                    split_hi(act, p.U + 2 * j + 1 + R, i, 1)
            loop(act, 2, gb)

            def qb(i):
                for j in range(4):
                    s, rnd = slot(p.U + 8 + j, i, 1)
                    act.wait_ge(unit_done[s], rnd + 2)
                    m = i * 4 + j
                    act.wait_ge(p.q_v.sem, p.q_v.past("q", m, 2))
                    ins = act.activation(raw[:, j % 2, 0:T], ps[:, s, 0:T], ACT.Copy)
                    ins.then_inc(acc_free[s], 1)
                    split_hi(act, p.U + 8 + j + R, i, 1)
            loop(act, 2, qb)
            Uv = p.U + 16
        else:
            for j in range(4):
                s, rnd = slot(p.U + j)
                act.wait_ge(unit_done[s], rnd + 2)
                if j >= 2:
                    act.wait_ge(p.q_v.sem, p.q_v.past("q", j - 2))
                ins = act.activation(raw[:, j % 2, 0:T], ps[:, s, 0:T], ACT.Copy)
                ins.then_inc(acc_free[s], 1)
                split_hi(act, p.U + j + R)
            Uv = p.U + 4
        for j in range(4):
            s, rnd = slot(Uv + j)
            act.wait_ge(unit_done[s], rnd + 2)
            if j >= 2:
                act.wait_ge(p.v_p.sem, p.v_p.past("t", j - 2))
            a = ps[:, s, 0:T]
            ins = act.activation(bycol(vraw[:, j % 2, 0:T]) if p.lat else vraw[:, j % 2, 0:T], grid(a) if p.lat else a, ACT.Copy)
            ins.then_inc(acc_free[s], 1)
            split_hi(act, Uv + j + R)

    def inproj_dve(dve, p, glu=True):
        T = p.T
        if glu:
            dve.memset(ub[:, :, 0:PADT], 0.0)
            dve.memset(ub[:, :, PADT + T:2 * PADT + T], 0.0)

            def gb(i):
                for j in range(2):
                    m = i * 2 + j
                    s, rnd = slot(p.U + 2 * j, i, 1)
                    dve.wait_ge(unit_done[s], rnd + 2)
                    dve.wait_ge(acc_free[(p.U + 2 * j + 1) % R], read_out(p.U + 2 * j + 1, i, 1))
                    ins = dve.tensor_tensor(ub[:, m, PADT:PADT + T], ps[:, s, 0:T], gs[:, j, 0:T], ALU.mult)
                    ins.then_inc(acc_free[s], 1)
            loop(dve, 2, gb)
        if p.lat:
            for part, dst in ((0, qT), (1, kT)):
                def qb(j2, part=part, dst=dst):
                    for jj in range(2):
                        j = j2 * 2 + jj
                        m = part * 4 + j
                        dve.wait_ge(p.q_p.sem, p.q_p.past("rot", m))
                        dve.tensor_tensor(rt[:, 0], raw[:, jj], cosT, ALU.mult)
                        dve.tensor_tensor(rt[:, 1], ps[:, 4 + jj, :], sinT, ALU.mult)
                        dve.drain()
                        if part == 0:
                            ins = dve.tensor_tensor(bycol(dst[:, j]), grid(rt[:, 0]), grid(rt[:, 1]), ALU.add)
                        else:
                            for a in range(2):
                                o = dst[:, j, 4 * P * a:4 * P * a + 2 * P].rearrange("p (c r) -> p c r", r=GH)
                                c = slice(32 * a, 32 * a + 32)
                                ins = dve.tensor_tensor(o, grid(rt[:, 0])[:, c], grid(rt[:, 1])[:, c], ALU.add)
                            dve.drain()
                            for m_, (lo, hi) in MIX.items():
                                dve.tensor_copy(dst[:, j, m_ * P:m_ * P + 64], dst[:, j, lo * P:lo * P + 64])
                                ins = dve.tensor_copy(dst[:, j, m_ * P + 64:m_ * P + P], dst[:, j, hi * P + 64:hi * P + P])
                        ins.then_inc(p.q_v.sem, 1)
                        dve.drain()
                loop(dve, 2, qb)
        else:
            for m in range(8 if glu else 4):
                dve.wait_ge(acc_free[(p.U + (8 if glu else 0) + m) % R], read_out(p.U + (8 if glu else 0) + m))
                k = m - 4 if glu else m
                dve.tensor_copy(qT[:, m, 0:T] if k < 0 else kctx[:, k], raw[:, m % 2, 0:T]).then_inc(p.q_v.sem, 1)
        for j in range(4):
            dve.wait_ge(p.v_p.sem, p.v_p.past("t", j))
            v = ps[:, 6 + j % 2, 0:T].rearrange("p (b d) -> p b d", d=P)
            c = slice(j * P, (j + 1) * P)
            if p.lat:
                dve.tensor_copy(vT[:, 0:2, c], v[:, 0:2])
                ins = dve.tensor_copy(vT[:, 4:6, c], v[:, 2:4])
            else:
                ins = dve.tensor_copy(vctx[:, :, c], v)
            ins.then_inc(p.v_v.sem, 1)
        dve.drain()
        if p.lat:
            for m_, (lo, hi) in MIX.items():
                dve.tensor_copy(vT[0:64, m_], vT[0:64, lo])
                dve.tensor_copy(vT[64:P, m_], vT[64:P, hi])
            dve.drain()

    def conv_pool(pool, p):
        T, l = p.T, p.l
        pool.wait_ge(acc_free[(p.U + 6) % R], read_out(p.U + 6))
        pool.wait_ge(p.q_v.sem, p.q_v.past("q", 7))
        for m in range(2):
            pool.tensor_scalar(co[:, m, 0:T], ub[:, m, 0:T], colr(f"dw{l}", 1, m), colr(f"dwb{l}", 1, m), ALU.mult, ALU.add)

        def tap(k):
            for m in range(2):
                o = co[:, m, 0:T]
                pool.drain()
                pool.tensor_tensor(ct[:, 0:T], ub[:, m, bass.ds(k + 1, T)], col(f"dw{l}", k * 4 + 4 + m).to_broadcast([P, T]), ALU.mult)
                pool.drain()
                ins = pool.tensor_tensor(o, o, ct[:, 0:T], ALU.add)
            ins.then_inc(p.c_g.sem, 1)
        loop(pool, POOL_TAPS - 1, tap)
        pool.drain()

    def conv_tap(dve, p, k, tiles=(2, 3)):
        for m in tiles:
            o = co[:, m, 0:p.T]
            dve.scalar_tensor_tensor(o, ub[:, m, bass.ds(k, p.T)], col(f"dw{p.l}", k * 4 + m), o, ALU.mult, ALU.add)

    def conv_dve(dve, p):
        T, l = p.T, p.l

        dve.wait_ge(p.c_g.sem, p.c_g.past("conv", POOL_TAPS - 2))
        def rest(k):
            conv_tap(dve, p, k + POOL_TAPS, (0, 1))
            dve.drain()
        loop(dve, KTAP - POOL_TAPS, rest)
        a = lmu[:, 0:T]
        dve.tensor_tensor(a, co[:, 0, 0:T], co[:, 1, 0:T], ALU.add)
        for m in (2, 3):
            dve.drain()
            ins = dve.tensor_tensor(a, a, co[:, m, 0:T], ALU.add)
        ins.then_inc(p.c_v.sem, 1)
        dve.wait_ge(p.c_p.sem, p.c_p.past("mu"))
        ins = dve.tensor_tensor(cn_(p), co[:, :, 0:T], ps[:, 7, 0:T].unsqueeze(1).to_broadcast([P, 4, T]), ALU.subtract)
        ins.then_inc(p.c_v.sem, 1)
        dve.wait_ge(p.c_a.sem, p.c_a.past("sq"))
        dve.tensor_tensor(a, lsq[:, 0, 0:T], lsq[:, 1, 0:T], ALU.add)
        for m in (2, 3):
            dve.drain()
            ins = dve.tensor_tensor(a, a, lsq[:, m, 0:T], ALU.add)
        ins.then_inc(p.c_v.sem, 1)
        dve.wait_ge(p.c_a.sem, p.c_a.past("root"))
        r = lrs[:, 0:T]
        dve.reciprocal(r, r)
        dve.drain()
        for m in range(4):
            ins = dve.scalar_tensor_tensor(lsq[:, m, 0:T], cn[:, m, 0:T], colr(f"lng{l}", 1, m), r, ALU.mult, ALU.mult)
        ins.then_inc(p.c_v.sem, 1)
        dve.wait_ge(p.c_a.sem, p.c_a.past("hi"))
        dve.tensor_tensor(hlo[:, 0:4, 0:T], cn_(p), hhi[:, 0:4, 0:T].bitcast(F32), ALU.subtract).then_inc(p.c_lo.sem, 1)

    def cn_(p):
        return cn[:, :, 0:p.T]

    def conv_act(act, p):
        T, l = p.T, p.l
        act.wait_ge(p.c_v.sem, p.c_v.past("cen"))
        act.activation(lsq[:, :, 0:T], cn_(p), ACT.Square).then_inc(p.c_a.sem, 1)
        act.wait_ge(p.c_p.sem, p.c_p.past("var"))
        act.activation(lrs[:, 0:T], ps[:, 7, 0:T], ACT.Sqrt, bias=col("eps6")).then_inc(p.c_a.sem, 1)
        act.wait_ge(p.c_v.sem, p.c_v.past("lo"))
        for m in range(4):
            ins = act.activation(cn[:, m, 0:T], lsq[:, m, 0:T], ACT.Silu, bias=colr(f"lnb{l}", 1, m))
        ins.then_inc(p.c_a.sem, 1)
        act.drain()
        act.activation(hhi[:, 0:4, 0:T], cn_(p), ACT.Copy).then_inc(p.c_a.sem, 1)

    def conv_pe(pe, p):
        T = p.T
        pe.wait_ge(p.c_v.sem, p.c_v.past("acc"))
        pe.matmul(ps[:, 7, 0:T], ones512, lmu[:, 0:T], start=True, stop=True).then_inc(p.c_p.sem, 1)
        pe.wait_ge(p.c_v.sem, p.c_v.past("t"))
        pe.matmul(ps[:, 7, 0:T], ones512, lmu[:, 0:T], start=True, stop=True).then_inc(p.c_p.sem, 1)

    def attn(p):
        return (4, SEQ, 4) if p.lat else (2, CTX, 2)

    def attn_pe(pe, p):
        nj, W, nb = attn(p)
        n = 2 * nj
        all_freed(pe, p.U + 20)

        def body(hp):
            pe.wait_ge(p.a_st.sem, p.a_st.past("st", hp))

            def scores(u):
                h, j = u // nj, u % nj
                d = slice(64 * h, 64 * h + 64)
                pe.wait_ge(p.a_exp.sem, p.a_exp.past("exp", hp * n + u, 2))
                qq = qst[d, j * P:(j + 1) * P]
                if p.lat:
                    w0 = WIN_AT[j] * P
                    pe.matmul(ps[:, 4 + u % 2, 0:2 * P], qq, kst[d, w0:w0 + 2 * P], start=True, stop=True)
                    last = pe.matmul(ps[:, 4 + u % 2, 2 * P:W], qq, kcs[d, :], start=True, stop=True)
                else:
                    last = pe.matmul(ps[:, 4 + u % 2, 0:W], qq, kcs[d, :], start=True, stop=True)
                last.then_inc(p.a_s.sem, 1)

            def turn(u):
                pe.wait_ge(p.a_exp.sem, p.a_exp.past("exp", hp * n + u))
                pe.wait_ge(p.a_pt.sem, p.a_pt.past("copied", hp * n + u, 2))
                for b in range(nb):
                    last = pe.transpose(ps[:, 6 + u % 2, b * P:(b + 1) * P], pex[:, u % 2, b * P:(b + 1) * P], ident)
                last.then_inc(p.a_turn.sem, 1)

            def values(u):
                h, j = u // nj, u % nj
                pe.wait_ge(p.a_pt.sem, p.a_pt.past("copied", hp * n + u))
                pe.wait_ge(p.a_out.sem, p.a_out.past("out", hp * n + u, 2))
                for b in range(nb):
                    c = bass.ds(hp * P + 64 * h, 64)
                    v = vctx[:, b - 2 if p.lat else b, c] if (not p.lat or b >= 2) else vT[:, WIN_AT[j] + b, c]
                    last = pe.matmul(ps[:, u % 2, 0:64], pT[:, u % 2, b * P:(b + 1) * P], v, start=b == 0, stop=b == nb - 1)
                last.then_inc(p.a_pv.sem, 1)

            scores(0)
            scores(1)
            for u in range(n + 1):
                if u < n:
                    turn(u)
                if u + 2 < n:
                    scores(u + 2)
                if u:
                    values(u - 1)
        pe.wait_ge(p.v_v.sem, p.v_v.past("v", 3))
        loop(pe, 4, body)
        for m in range(4):
            pe.wait_ge(p.a_out.sem, p.a_out.past("out", 4 * n - 1))
            if m >= 2:
                pe.wait_ge(p.o_v.sem, p.o_v.past("lo", m - 2))
            for j in range(nj):
                last = pe.transpose(ps[:, 6 + m % 2, j * P:(j + 1) * P], osb[:, j, m * P:(m + 1) * P], ident)
            last.then_inc(p.o_p.sem, 1)
        pe.wait_ge(p.o_v.sem, p.o_v.past("lo", 3))

    def attn_act(act, p):
        nj, W, nb = attn(p)
        n = 2 * nj
        act.wait_ge(p.v_p.sem, p.v_p.past("t", 3))

        def body(hp):
            if p.lat:
                act.wait_ge(p.a_max.sem, p.a_max.past("max", hp * n, 1))
                act.dma_start(biasb[:, :], A["attn_bias"][p.l, hp]).then_inc(s_bias, 16)
            def exps(u):
                act.wait_ge(p.a_max.sem, p.a_max.past("max", hp * n + u))
                act.wait_ge(p.a_out.sem, p.a_out.past("out", hp * n + u, 4))
                act.activation(pex[:, u % 2, 0:W], ps[:, 4 + u % 2, 0:W], ACT.Exp, bias=sm[:, 0, u % 4:u % 4 + 1],
                               accum_out=sm[:, 1, u % 4:u % 4 + 1]).then_inc(p.a_exp.sem, 1)

            exps(0)
            for u in range(n):
                if u + 1 < n:
                    exps(u + 1)
                act.wait_ge(p.a_turn.sem, p.a_turn.past("turned", hp * n + u))
                act.wait_ge(p.a_pv.sem, p.a_pv.past("values", hp * n + u, 2))
                act.activation(pT[:, u % 2, 0:W], ps[:, 6 + u % 2, 0:W], ACT.Copy).then_inc(p.a_pt.sem, 1)
        loop(act, 4, body)
        for m in range(4):
            act.wait_ge(p.o_p.sem, p.o_p.past("t", m))
            src = ps[:, 6 + m % 2, 0:p.T]
            o = hhi[:, 4 + m, 0:p.T]
            act.activation(grid(o) if p.lat else o, bycol(src) if p.lat else src, ACT.Copy).then_inc(p.o_a.sem, 1)

    def attn_dve(dve, p):
        nj, W, nb = attn(p)
        n = 2 * nj
        for m in (2, 3):
            dve.tensor_scalar(co[:, m, 0:p.T], ub[:, m, 0:p.T], colr(f"dw{p.l}", 1, m), colr(f"dwb{p.l}", 1, m), ALU.mult, ALU.add)
        for k in range(1, KTAP - 28):
            dve.drain()
            conv_tap(dve, p, k)

        def body(hp):
            dve.wait_ge(p.a_s.sem, p.a_s.past("scores", hp * n, 1))
            dve.tensor_scalar(qst[:, 0:p.T], qT[:, hp, 0:p.T], DH ** -0.5, None, ALU.mult)
            if p.lat:
                dve.tensor_copy(kst[:, :], kT[:, hp])
            dve.tensor_copy(kcs[:, :], kctx[:, hp]).then_inc(p.a_st.sem, 1)
            if p.lat:
                dve.wait_ge(s_bias, p.bias0 + (hp + 1) * 16)

            def top(u):
                h, j = u // nj, u % nj
                dve.wait_ge(p.a_s.sem, p.a_s.past("scores", hp * n + u))
                dve.wait_ge(p.a_exp.sem, p.a_exp.past("exp", hp * n + u, 2))
                if p.lat:
                    w = ps[:, 4 + u % 2, 0:2 * P]
                    dve.tensor_tensor(w, w, biasb[:, h, j], ALU.add)
                    dve.drain()
                dve.tensor_reduce(sm[:, 0, u % 4:u % 4 + 1], ps[:, 4 + u % 2, 0:W], AX.X, ALU.max, negate=True).then_inc(p.a_max.sem, 1)

            def outp(u):
                h, j = u // nj, u % nj
                dve.wait_ge(p.a_exp.sem, p.a_exp.past("exp", hp * n + u))
                dve.reciprocal(sm[:, 2, u % 4:u % 4 + 1], sm[:, 1, u % 4:u % 4 + 1])
                for k in range(u * 7 // n, (u + 1) * 7 // n):
                    if k > u * 7 // n:
                        dve.drain()
                    conv_tap(dve, p, hp * 7 + (k + KTAP - 28))
                dve.drain()
                dve.wait_ge(p.a_pv.sem, p.a_pv.past("values", hp * n + u))
                dve.tensor_scalar(osb[:, j, bass.ds(hp * P + 64 * h, 64)], ps[:, u % 2, 0:64],
                                               sm[:, 2, u % 4:u % 4 + 1], None, ALU.mult).then_inc(p.a_out.sem, 1)
            top(0)
            top(1)
            for u in range(n):
                if u + 2 < n:
                    top(u + 2)
                outp(u)
            dve.drain()
        loop(dve, 4, body)
        for m in range(4):
            dve.wait_ge(p.o_a.sem, p.o_a.past("hi", m))
            if m == 3:
                dve.wait_ge(p.c_g.sem, p.c_g.past("conv", POOL_TAPS - 2))
            src = ps[:, 6 + m % 2, 0:p.T]
            o, h = hlo[:, 4 + m, 0:p.T], hhi[:, 4 + m, 0:p.T].bitcast(F32)
            if p.lat:
                o, h, src = grid(o), grid(h), bycol(src)
            dve.tensor_tensor(o, src, h, ALU.subtract).then_inc(p.o_v.sem, 1)

    def gates_pe(pe, p):
        pe.wait_ge(p.a_out.sem, p.a_out.past("out", 4 * 2 * attn(p)[0] - 1))
        loop(pe, 4, lambda i: [pe_unit(pe, p.U + 20 + j, i, 1, xhi, xlo, p.T) for j in range(4)])

    def gates_act(act, p):
        def body(i):
            for j in range(4):
                s, rnd = slot(p.U + 20 + j, i, 1)
                act.wait_ge(unit_done[s], rnd + 2)
                act.activation(gt[:, i * 4 + j, 0:p.T], ps[:, s, 0:p.T], ACT.Sigmoid).then_inc(acc_free[s], 1)
                split_hi(act, p.U + 20 + j + R, i, 1)
        loop(act, 4, body)

    def merge_pe(pe, p):
        pe.wait_ge(p.c_lo.sem, p.c_lo.past("lo"))
        loop(pe, 2, lambda i: [pe_unit(pe, p.U + 36 + j, i, 1, hhi, hlo, p.T, dual=True) for j in range(4)])

    def merge_act(act, p):
        def body(i):
            for j in range(4):
                m = i * 4 + j
                split_hi(act, p.U + 36 + j + R, i, 1)
                act.wait_ge(p.m_v.sem, p.m_v.past("v", m))
                act.activation(mhi[:, m, 0:p.T], mv[:, j % 2, 0:p.T], ACT.Copy).then_inc(p.m_h.sem, 1)
        loop(act, 2, body)

    def merge_dve(dve, p):
        T = p.T
        all_freed(dve, p.U + 36)

        def body(i):
            for j in range(4):
                m = i * 4 + j
                s, rnd = slot(p.U + 36 + j, i, 1)
                dve.wait_ge(unit_done[s], rnd + 2)
                gc, ga = gt[:, m, 0:T], gt[:, m + NT, 0:T]
                dve.tensor_tensor(gc, ps[:, s, 0:T], gc, ALU.mult)
                dve.tensor_tensor(ga, ps[:, s + R, 0:T], ga, ALU.mult).then_inc(acc_free[s], 1)
                dve.drain()
                v = mv[:, j % 2, 0:T]
                dve.tensor_tensor(v, gc, ga, ALU.add).then_inc(p.m_v.sem, 1)
                dve.wait_ge(p.m_h.sem, p.m_h.past("hi", m))
                dve.tensor_tensor(mlo[:, m, 0:T], v, mhi[:, m, 0:T].bitcast(F32), ALU.subtract).then_inc(p.m_v.sem, 1)
        loop(dve, 2, body)

    def ffn_units(p):
        U = p.U + 52
        for t0, n in CHUNKS2:
            yield U, U + 2 * n, t0, n
            U += 2 * n + 8

    def ffn_pe(pe, p):
        n1 = p.norm(1)
        for kt in range(NT):
            pe.wait_ge(n_lo.sem, n_lo.past("lo", hi_before[n1] + kt))
        for U, D, t0, n in ffn_units(p):
            loop(pe, n // 2, lambda i: [pe_unit(pe, U + j, i, 1, xhi, xlo, p.T) for j in range(4)])
            for kt in range(n):
                pe.wait_ge(p.f_v.sem, p.f_v.past("lo", t0 + kt))
            loop(pe, 2, lambda i: [pe_unit(pe, D + j, i, 1, hhi, hlo, p.T, n) for j in range(4)])

    def ffn_act(act, p):
        T, l = p.T, p.l
        for U, D, t0, n in ffn_units(p):
            def body(i):
                for j in range(2):
                    t = i * 2 + (t0 + j)
                    for k, name in enumerate("ag"):
                        s, rnd = slot(U + 2 * j + k, i, 1)
                        act.wait_ge(unit_done[s], rnd + 2)
                        act.wait_ge(p.f_v.sem, p.f_v.past("h", t, 2))
                        act.activation(fa[:, j, k, 0:T], ps[:, s, 0:T], ACT.Identity,
                                                 scale=col(f"fw1{l}", t + 22 * k), bias=col(f"fb{l}", t + 22 * k)).then_inc(p.f_a.sem, 1)
                        split_hi(act, U + 2 * j + k + R, i, 1)
                    act.wait_ge(acc_free[(U + 2 * j + 1) % R], read_out(U + 2 * j + 1, i, 1))
                    act.activation(fs[:, j, 0, 0:T], fa[:, j, 1, 0:T], ACT.Silu).then_inc(p.f_h.sem, 1)
                    act.wait_ge(p.f_v.sem, p.f_v.past("h", t))
                    act.activation(hhi[:, i * 2 + j, 0:T], fs[:, j, 1, 0:T], ACT.Copy).then_inc(p.f_h.sem, 1)
            loop(act, n // 2, body)
            act_units(act, D, 2)

    def ffn_dve(dve, p, last=False):
        T, l = p.T, p.l
        for U, D, t0, n in ffn_units(p):
            def body(i):
                for j in range(2):
                    t = i * 2 + (t0 + j)
                    for k, name in enumerate("ag"):
                        s = slot(U + 2 * j + k)[0]
                        dve.wait_ge(p.f_a.sem, p.f_a.past(name, t))
                        o = fa[:, j, k]
                        dve.scalar_tensor_tensor(o[:, 1:T], ps[:, s, 0:T - 1], col(f"fw0{l}", t + 22 * k), o[:, 1:T], ALU.mult, ALU.add)
                        dve.drain()
                        ins = dve.scalar_tensor_tensor(o[:, 0:T - 1], ps[:, s, 1:T], col(f"fw2{l}", t + 22 * k), o[:, 0:T - 1], ALU.mult, ALU.add)
                        ins.then_inc(acc_free[s], 1)
                    dve.wait_ge(p.f_h.sem, p.f_h.past("silu", t))
                    dve.tensor_tensor(fs[:, j, 1, 0:T], fs[:, j, 0, 0:T], fa[:, j, 0, 0:T], ALU.mult).then_inc(p.f_v.sem, 1)
                    dve.wait_ge(p.f_h.sem, p.f_h.past("hi", t))
                    h = i * 2 + j
                    dve.tensor_tensor(hlo[:, h, 0:T], fs[:, j, 1, 0:T], hhi[:, h, 0:T].bitcast(F32), ALU.subtract).then_inc(p.f_v.sem, 1)
            loop(dve, n // 2, body)
            add_dve(dve, D, 2, p.res, T, gate=p.modv(5))

    passes = [Pass("c0", 0, False, N_B1), Pass("l0", 0, True, N_B1 + N_LAYER),
              Pass("c1", 1, False, U_KV), Pass("l1", 1, True, U_KV + 8)]
    assert N_UNITS == U_KV + 8 + N_LAYER
    added = {"c0b": N_B1 + 44, "c1a": N_B1 + N_LAYER - 8, "l0b": N_B1 + N_LAYER + 44,
             "l1a": U_KV - 8, "l1b": U_KV + 8 + 44}
    s_x = sem("x_landed")
    s_c = sem("ctx_landed")

    def ready_of(name):
        def ready(eng, kt):
            if name == "c0a":
                eng.wait_ge(s_c, 16)
            elif name == "l0a":
                eng.wait_ge(n_fin.sem, n_fin.past("fin", NT - 1))
            else:
                eng.wait_ge(acc_free[(added[name] + kt) % R], read_out(added[name] + kt))
        return ready

    def norm_all(eng, p, k):
        name = p.key + "ab"[k]
        n = NORM[name]
        shift = p.modv(3 * k)
        if eng == "act":
            return lambda act: norm_act(act, n, p.src, p.T, "eps6", ready_of(name), True, shift)
        if eng == "pe":
            return lambda pe: norm_pe(pe, n, p.T)
        return lambda dve: norm_dve(dve, n, p.src, p.T, p.gain(k), True, shift)

    g1 = lambda name: (lambda kt: colr(name, 1, kt))
    rsrc = lambda kt: res[:, kt]

    with nc.Block() as setup:
        @setup.gpsimd
        def _(pool):
            for s in every_steps:
                s.credit(pool)
            for s in range(R):
                pool.nop().then_inc(unit_done[s], 1)
                pool.nop().then_inc(acc_free[s], 1)
            pool.nop().then_inc(f_d, 128)

    with nc.Block() as block:
        @block.sync
        def _(sp):
            sp.dma_start(xin[:, :], A["x0T"]).then_inc(s_in, 16)
            sp.dma_start(vec[:, :], A["vecs"]).then_inc(s_cst, 16)
            sp.dma_start(cst[:, :], A["consts"]).then_inc(s_cst, 16)

            def load(g, row, i=0, rb=0):
                s = g % R
                if g >= R:
                    sp.wait_ge(lo_done[s], raw_round(g, i, rb))
                sp.dma_start(wraw[:, s], A["stream"][row]).then_inc(landed[s], 16)

            def segment(g, row, n):
                loop(sp, n // R, lambda i: [load(g + j, i * R + (row + j), i, 1) for j in range(R)])
                for j in range(n - n % R, n):
                    load(g + j, row + j)

            for g in range(R):
                load(g, g)
            segment(R, R, U_ADA - R)

            def ada(i):
                for j in range(R):
                    s, rnd = slot(U_ADA + j, i, 1)
                    sp.wait_ge(lo_done[s], rnd)
                    sp.dma_start(wraw[:, s], A["w_ada"][i * R + j]).then_inc(landed[s], 16)
            loop(sp, N_ADA // R, ada)
            segment(U_ADA, U_ADA, N_B1 - U_ADA)
            segment(N_B1, N_B1, N_LAYER)
            segment(N_B1 + N_LAYER, N_B1, N_LAYER)
            segment(U_KV, N_B1 + N_LAYER + 12, 8)
            segment(U_KV + 8, N_B1 + N_LAYER, N_LAYER)
            sp.wait_ge(n_fin.sem, n_fin.past("fin", 2 * NT - 1))
            sp.dma_start(out, res[:, :]).then_inc(s_out, 16)
            sp.wait_ge(s_out, 16)

        @block.tensor
        def _(pe):
            pe.wait_ge(s_cst, 32)
            norm_pe(pe, NORM["mix"], TM)
            proj_pe(pe)
            ssd_pe(pe)
            norm_pe(pe, NORM["ssd"], SEQ)
            pe.wait_ge(d_v.sem, d_v.past("state", NCH - 1))
            add_pe(pe, U_OUT1, 2, hhi, hlo, SEQ, ready=normed("ssd")(pe))
            s5_pe(pe)
            for kt in range(NT):
                pe.wait_ge(f_v.sem, f_v.past("lo", kt))
            pe.wait_ge(f_a.sem, f_a.past("ada", NT - 1))
            pairs_pe(pe, U_GLU, 4, hhi, hlo, SEQ)
            norm_pe(pe, NORM["s5"], SEQ)
            add_pe(pe, U_OUT2, 2, xhi, xlo, SEQ, ready=normed("s5")(pe))
            norm_pe(pe, NORM["mlp"], SEQ)
            mlp_pe(pe)
            norm_pe(pe, NORM["final1"], SEQ)
            for p in passes:
                full = p.key != "c1"
                norm_all("pe", p, 0)(pe)
                inproj_pe(pe, p, full)
                if full:
                    attn_pe(pe, p)
                    gates_pe(pe, p)
                    conv_pe(pe, p)
                    merge_pe(pe, p)
                    add_pe(pe, p.U + 44, 2, mhi, mlo, p.T, ready=lambda kt: pe.wait_ge(p.m_v.sem, p.m_v.past("lo", kt)))
                    norm_all("pe", p, 1)(pe)
                    ffn_pe(pe, p)
            norm_pe(pe, NORM["final2"], SEQ)

        @block.scalar
        def _(act):
            act.wait_ge(s_cst, 32)
            act.activation(cs[:, :], colr("c", 16).rearrange("p (k c) -> p k c", c=2), ACT.Silu).then_inc(s_cs, 1)
            act.wait_ge(s_in, 16)
            norm_act(act, NORM["mix"], lambda kt: xin[:, kt], TM, "eps5")
            for g in range(R):
                split_hi(act, g)
            proj_act(act)
            ssd_act(act)
            act.wait_ge(d_p.sem, d_p.past("y", NCH - 1))
            act.wait_ge(d_v.sem, d_v.past("state", NCH - 1))
            act.dma_start(res[:, :], A["x0T"][:, :, N_META:]).then_inc(s_x, 16)
            norm_act(act, NORM["ssd"], ysrc, SEQ, "eps5", ready=lambda e, kt: e.wait_ge(s_yg.sem, s_yg.past("gated")), dst=(hhi, hlo))
            act.wait_ge(n_lo.sem, n_lo.past("lo", 2 * NT - 1))
            act.dma_start(pm[:, 0:3], A["s5_lam"]).then_inc(s_5in, 16)
            act.dma_start(bc5[:, :], A["s5_bc"]).then_inc(s_5in, 16)
            act.dma_start(d5[:, :], A["s5_d"]).then_inc(s_5in, 16)
            act_units(act, U_OUT1, 2)
            s5_param_act(act)
            s5_act(act)
            glu_act(act)
            norm_act(act, NORM["s5"], lambda kt: s5o[:, kt], SEQ, "eps5", ready=lambda e, kt: e.wait_ge(acc_free[(U_GLU + 2 * kt) % R], read_out(U_GLU + 2 * kt)))
            act_units(act, U_OUT2, 2)
            norm_act(act, NORM["mlp"], rsrc, SEQ, "eps5", ready=lambda e, kt: e.wait_ge(acc_free[(U_OUT2 + kt) % R], read_out(U_OUT2 + kt)))
            mlp_act(act)
            norm_act(act, NORM["final1"], rsrc, SEQ, "eps5", ready=lambda e, kt: e.wait_ge(acc_free[(N_B1 - 8 + kt) % R], read_out(N_B1 - 8 + kt)), split=False)
            act.dma_start(resc[:, :], A["ctxT"]).then_inc(s_c, 16)
            for p in passes:
                full = p.key != "c1"
                norm_all("act", p, 0)(act)
                inproj_act(act, p, full)
                if full:
                    attn_act(act, p)
                    gates_act(act, p)
                    conv_act(act, p)
                    merge_act(act, p)
                    act_units(act, p.U + 44, 2)
                    norm_all("act", p, 1)(act)
                    ffn_act(act, p)
            norm_act(act, NORM["final2"], rsrc, SEQ, "eps6", ready=lambda e, kt: e.wait_ge(acc_free[(N_UNITS - 8 + kt) % R], read_out(N_UNITS - 8 + kt)), split=False)

        @block.vector
        def _(dve):
            dve.wait_ge(s_cst, 32)
            dve.wait_ge(s_in, 16)
            norm_dve(dve, NORM["mix"], lambda kt: xin[:, kt], TM, g1("g_mix"))
            proj_dve(dve)
            ssd_dve(dve)
            norm_dve(dve, NORM["ssd"], ysrc, SEQ, g1("g_ssd"), dst=(hhi, hlo))
            dve.wait_ge(s_x, 16)
            add_dve(dve, U_OUT1, 2, res, SEQ)
            s5_param_dve(dve)
            s5_dve(dve)
            ada_dve(dve)
            glu_dve(dve)
            norm_dve(dve, NORM["s5"], lambda kt: s5o[:, kt], SEQ, g1("g_s5"))
            add_dve(dve, U_OUT2, 2, res, SEQ)
            norm_dve(dve, NORM["mlp"], rsrc, SEQ, g1("g_mlp"))
            mlp_dve(dve)
            norm_dve(dve, NORM["final1"], rsrc, SEQ, g1("g_final"), split=False)
            dve.drain()
            for p in passes:
                full = p.key != "c1"
                norm_all("dve", p, 0)(dve)
                inproj_dve(dve, p, full)
                if full:
                    attn_dve(dve, p)
                    conv_dve(dve, p)
                    merge_dve(dve, p)
                    add_dve(dve, p.U + 44, 2, p.res, p.T, gate=p.modv(2))
                    norm_all("dve", p, 1)(dve)
                    ffn_dve(dve, p)
            norm_dve(dve, NORM["final2"], rsrc, SEQ, g1("gf2"), split=False)

        @block.gpsimd
        def _(pool):
            for g in range(R):
                split_lo(pool, g)
            pool_units(pool, U_U, 2)
            split_lo(pool, U_DT + R)
            pool_units(pool, U_XBC, 5)
            ssd_pool(pool)
            pool_units(pool, U_OUT1, 2)
            pool_units(pool, U_GLU, (N_B1 - U_GLU) // R)
            for p in passes:
                if p.key == "c1":
                    pool_units(pool, p.U, 2)
                else:
                    pool_units(pool, p.U, 5)
                    conv_pool(pool, p)
                    pool_units(pool, p.U + 20, 24 if p is passes[-1] else 25)


def consts():
    c = np.zeros((P, NCONST), np.float32)
    i = np.arange(P)
    c[:, CONST["ident"]:][:, :P] = np.eye(P)
    c[:, CONST["ones"]:][:, :P] = 1 / DM
    c[:, CONST["ones512"]:][:, :P] = 1 / CONV
    c[:, CONST["tri"]:][:, :P] = i[:, None] <= i[None, :]
    r = np.zeros((P, P))
    for m in range(P):
        if m % 32 < 16:
            r[m + 16, m] = -1
        else:
            r[m - 16, m] = 1
    c[:, CONST["rot"]:][:, :P] = r
    half = DH // 2
    inv = (np.float32(10000.0) ** (-np.arange(0, half, 2, dtype=np.float32) / half)).astype(np.float32)
    t = np.arange(SEQ)
    pos = np.where((i % DH < half)[:, None], (t // GW)[None], (t % GW)[None]).astype(np.float32)
    ang = (pos * inv[i % 16][:, None]).astype(np.float32)
    c[:, CONST["cos"]:][:, :SEQ] = np.cos(ang)
    c[:, CONST["sin"]:][:, :SEQ] = np.sin(ang)
    c[0:16, CONST["keep"]:] = np.arange(NCH * CHUNK) % CHUNK != 0
    return c


def tiles(w):
    k, m = w.shape
    return w.reshape(k // P, P, m // P, P).transpose(2, 1, 0, 3)


def rows_of_512(w):
    n, k, m = w.shape
    return w.reshape(n, k // 256, 2, P, m // 512, 512).transpose(0, 4, 1, 3, 2, 5).reshape(-1, P, 8, P)


def unit_stream(a):
    units = []

    def add(w):
        w = w.reshape(P, -1)
        if w.shape[1] < 8 * P:
            w = np.concatenate([w, np.zeros((P, 8 * P - w.shape[1]), w.dtype)], 1)
        units.append(w)

    w = a["w_in"][0]
    o_dt = DM + XBC_TILES * P
    dt = np.concatenate([w[:, o_dt:o_dt + 16], np.zeros((DM, P - 16), w.dtype)], 1)
    for part in (w[:, o_dt + 16:], dt, w[:, DM:o_dt], w[:, :DM]):
        for u in tiles(part):
            add(u)
    wo, glu = a["w_out"][0], tiles(a["w_glu"][0])
    for u in tiles(wo[:DM]):
        add(u)
    for m in range(NT):
        add(glu[m])
        add(glu[m + NT])
    for u in tiles(wo[DM:]):
        add(u)
    up = tiles(a["w_up"][0])
    for c in range(4):
        for m in range(8):
            add(up[c * 8 + m])
        for u in tiles(a["w_down"][0][c * DM:(c + 1) * DM]):
            add(u)
    assert len(units) == N_B1
    for l in range(2):
        w = tiles(a["w_in_2"][l])
        for m in range(4):
            add(w[m])
            add(w[m + 4])
        for m in range(8, 20):
            add(w[m])
        co, na = tiles(a["w_conv_out_2"][l]), tiles(a["w_na_out_2"][l])
        for m in range(20, 36):
            add(w[m])
        for m in range(NT):
            add(np.concatenate([co[m], na[m]], 1))
        for u in tiles(a["w_out_2"][l]):
            add(u)
        up = tiles(a["w_up_2"][l])
        for t0, n in CHUNKS2:
            for t in range(t0, t0 + n):
                add(up[t])
                add(up[t + FF2_TILES])
            for u in tiles(a["w_down_2"][l][t0 * P:(t0 + n) * P]):
                add(u)
    return np.stack(units).reshape(-1, P, 8, P)


def packed_vectors(a):
    v = np.zeros((P, NVEC), np.float32)

    def put(name, x):
        o, n = VEC[name]
        v[:, o:o + n] = np.asarray(x).reshape(n, P).T

    def pad(x):
        return np.concatenate([x, np.zeros(P - len(x), x.dtype)])

    for name, key in (("g_mix", "g_mix"), ("cb", "conv_b"), ("g_ssd", "g_ssd"), ("b_glu", "b_glu"), ("g_s5", "g_s5"), ("g_mlp", "g_mlp")):
        put(name, a[key][0])
    for k in range(4):
        put(f"cw{k}", a["conv_w"][0, k])
    put("dtb", pad(a["dt_bias"][0]))
    put("alog", pad(a["a_log"][0]))
    put("dskip", np.repeat(a["d_ssd"][0], HEAD))
    put("g_final", a["g_final"])
    put("gf2", a["final_norm_g_2"])
    v[:, VEC["c"][0]:][:, :16] = np.stack([a["c_2"][0].reshape(8, P), a["c_ctx_2"].reshape(8, P)], 1).reshape(16, P).T
    v[:, VEC["eps5"][0]] = 1e-5
    v[:, VEC["eps6"][0]] = 1e-6
    v[:, VEC["halfpi"][0]] = math.pi / 2
    v[:, VEC["one"][0]] = 1.0
    for l in range(2):
        put(f"bada{l}", a["b_ada_2"][l])
        put(f"n1{l}", a["norm1_g_2"][l])
        put(f"n2{l}", a["norm2_g_2"][l])
        put(f"dw{l}", a["conv_dw_2"][l])
        put(f"dwb{l}", a["conv_dw_b_2"][l])
        put(f"lng{l}", a["conv_ln_g_2"][l])
        put(f"lnb{l}", a["conv_ln_b_2"][l])
        for k in range(3):
            put(f"fw{k}{l}", a["ffn_dw_2"][l, k])
        put(f"fb{l}", a["ffn_dw_b_2"][l])
    return v


def window_bias(rpb):
    tile0 = [np.arange(16 * t, 16 * t + 16) for t in range(4)]
    stored = [tile0[0], tile0[1], None, None, tile0[2], tile0[3]]
    for m, (lo, hi) in MIX.items():
        stored[m] = np.concatenate([stored[lo][:8], stored[hi][8:]])
    rows = np.arange(GH)
    b = np.full((2, NH, 4, P, 2 * P), NEG, np.float32)
    for j in range(4):
        qc, qr = np.repeat(tile0[j], GH), np.tile(rows, 16)
        kc = np.concatenate([stored[WIN_AT[j]], stored[WIN_AT[j] + 1]])
        kc, kr = np.repeat(kc, GH), np.tile(rows, 32)
        start = np.clip(qc - 8, 0, GW - 16)
        inside = (kc[None] >= start[:, None]) & (kc[None] < start[:, None] + 16)
        dr = kr[None] - qr[:, None] + 7
        dc = np.where(inside, kc[None] - qc[:, None] + 15, 0)
        b[:, :, j] = np.where(inside, rpb[:, :, dr, dc], np.float32(NEG))
    return b.reshape(2, 4, 2, 4, P, 2 * P).transpose(0, 1, 4, 2, 3, 5)


def arrays_of(a):
    a = {k: np.asarray(v) for k, v in a.items()}
    h0 = np.concatenate([a["meta_tokens"], a["x"][0]], 0)
    fm = lambda x: x.T.reshape(-1, P, x.shape[0]).transpose(1, 0, 2)
    pair = lambda x: x.reshape(NPAIR, P).T
    lam = np.stack([pair(a["lam_re"][0]), pair(a["lam_im"][0]), pair(np.repeat(a["log_step"][0], S5_P))], 1)
    b = [a[k][0].reshape(NPAIR, P, S5_H).transpose(1, 0, 2) for k in ("b_re", "b_im")]
    c = [a[k][0].transpose(0, 2, 1).reshape(NPAIR, P, S5_H).transpose(1, 0, 2) for k in ("c_re", "c_im")]
    out = {
        "x0T": fm(h0), "ctxT": fm(a["ctx_2"][0]), "vecs": packed_vectors(a), "consts": consts(),
        "stream": unit_stream(a), "w_ada": rows_of_512(a["w_ada_2"]),
        "attn_bias": window_bias(a["na_rpb_2"]), "s5_lam": lam, "s5_bc": np.stack(b + c, 1), "s5_d": a["d_s5"][0].T,
    }
    return {k: np.ascontiguousarray(v) for k, v in out.items()}


def kernel(**inputs):
    import concourse.bacc as bacc
    from concourse.bass_utils import run_bass_kernel_spmd

    nc = bacc.Bacc("TRN2", target_bir_lowering=False, num_devices=1)
    arrays = arrays_of(inputs)
    A = {k: nc.dram_tensor(k, v.shape, F32, kind="ExternalInput").ap() for k, v in arrays.items()}
    out = nc.dram_tensor("outT", (P, NT, SEQ), F32, kind="ExternalOutput").ap()
    build(nc, A, out)
    r = run_bass_kernel_spmd(nc, [arrays], core_ids=[0])
    got = r.results[0]["outT"]
    return np.ascontiguousarray(got.transpose(2, 1, 0)).reshape(1, SEQ, DM)
```
